# Optimizing a Trainium2 kernel written in Bass

```python
import math
import jax
import jax.numpy as jnp
from jax import lax
import numpy as np
import jax, jax.numpy as jnp

D_MODEL = 1024
BATCH = 1
SEQ = 256
DEPTH = 1

D_MIX = D_MODEL
D_CONV = D_MIX // 2
CONV_GROUPS = 8
D_GLA = D_MIX - D_CONV
GLA_HEADS = 4
HEAD_V = D_GLA // GLA_HEADS
HEAD_K = HEAD_V // 2
D_GLA_K = GLA_HEADS * HEAD_K
GATE_RANK = 16
GATE_NORMALIZER = 16.0
CHUNK = 64
D_FF = 2816
CONV_WIDTH = 3
EPS = 1e-6
SPLIT_SIZES = (D_CONV, D_CONV, D_CONV,
               D_GLA_K, D_GLA_K, D_GLA, D_GLA,
               GATE_RANK, GATE_RANK)
D_IN = sum(SPLIT_SIZES)


def rmsnorm(x, g):
    xf = x.astype(jnp.float32)
    y = xf * lax.rsqrt(jnp.mean(xf * xf, axis=-1, keepdims=True) + EPS)
    return (y * g.astype(jnp.float32)).astype(x.dtype)

def dwconv3(x, w):
    xp = jnp.pad(x, ((0, 0), (1, 1), (0, 0)))
    return w[0] * xp[:, :-2] + w[1] * xp[:, 1:-1] + w[2] * xp[:, 2:]

def split_cols(p):
    idx, acc = [], 0
    for s in SPLIT_SIZES[:-1]:
        acc += s
        idx.append(acc)
    return jnp.split(p, idx, axis=-1)

def gla_chunked(q, k, v, log_a):
    b_, h_, L, dk = q.shape
    dv = v.shape[-1]
    n = L // CHUNK
    q = q.reshape(b_, h_, n, CHUNK, dk)
    k = k.reshape(b_, h_, n, CHUNK, dk)
    v = v.reshape(b_, h_, n, CHUNK, dv)
    cum = jnp.cumsum(log_a.reshape(b_, h_, n, CHUNK, dk), axis=3)
    cum_last = cum[:, :, :, -1:, :]
    q_in = q * jnp.exp(cum)
    k_in = k * jnp.exp(-cum)
    k_out = k * jnp.exp(cum_last - cum)
    mask = jnp.tril(jnp.ones((CHUNK, CHUNK), dtype=bool))
    scores = jnp.einsum('bhnid,bhnjd->bhnij', q_in, k_in)
    scores = jnp.where(mask, scores, 0.0)
    o_intra = jnp.einsum('bhnij,bhnje->bhnie', scores, v)
    kv = jnp.einsum('bhnjd,bhnje->bhnde', k_out, v)
    decay = jnp.exp(cum_last[:, :, :, 0, :])

    def step(state, inp):
        d_n, kv_n = inp
        return d_n[..., None] * state + kv_n, state

    _, s_prev = lax.scan(step, jnp.zeros((b_, h_, dk, dv), jnp.float32),
                         (jnp.moveaxis(decay, 2, 0), jnp.moveaxis(kv, 2, 0)))
    s_prev = jnp.moveaxis(s_prev, 0, 2)
    o_inter = jnp.einsum('bhnid,bhnde->bhnie', q_in, s_prev)
    return (o_intra + o_inter).reshape(b_, h_, L, dv)

def to_heads(t, d_head):
    b_, L, _ = t.shape
    return t.reshape(b_, L, -1, d_head).transpose(0, 2, 1, 3)

def gate_log_decay(lr, w_up, bias):
    pre = (lr @ w_up + bias).astype(jnp.float32)
    return jax.nn.log_sigmoid(pre) / GATE_NORMALIZER

def mixer(h, w_in, conv_a, gate_up_fwd, gate_bias_fwd, gate_up_bwd, gate_bias_bwd,
          gla_head_norm, w_out):
    p = h @ w_in
    gb, gc, gv, q, k, v, go, lr_f, lr_b = split_cols(p)
    y_a = gb * dwconv3(gc * gv, conv_a)
    la_f = gate_log_decay(lr_f, gate_up_fwd, gate_bias_fwd)
    la_b = gate_log_decay(lr_b, gate_up_bwd, gate_bias_bwd)
    qh = to_heads(q, HEAD_K).astype(jnp.float32) * (HEAD_K ** -0.5)
    kh = to_heads(k, HEAD_K).astype(jnp.float32)
    vh = to_heads(v, HEAD_V).astype(jnp.float32)
    af = to_heads(la_f, HEAD_K)
    ab = to_heads(la_b, HEAD_K)
    flip = lambda t: jnp.flip(t, axis=2)
    o_f = gla_chunked(qh, kh, vh, af)
    o_b = flip(gla_chunked(flip(qh), flip(kh), flip(vh), flip(ab)))
    o = o_f + o_b
    o = o * lax.rsqrt(jnp.mean(o * o, axis=-1, keepdims=True) + EPS) * gla_head_norm.astype(jnp.float32)
    b_, _, L, _ = o.shape
    o = o.transpose(0, 2, 1, 3).reshape(b_, L, D_GLA).astype(h.dtype)
    y_b = jax.nn.silu(go) * o
    y = jnp.concatenate([y_a, y_b], axis=-1)
    return y @ w_out

def conv_mlp(h, w_up, conv_w, w_down):
    u = dwconv3(h @ w_up, conv_w)
    gate, val = jnp.split(u, 2, axis=-1)
    return (jax.nn.silu(gate) * val) @ w_down

def first_inputs(seed: int = 0) -> dict:
    key = jax.random.key(seed)
    ks = jax.random.split(key, 20)
    f32 = jnp.float32
    nrm = lambda k, shape, scale: jax.random.normal(k, shape, f32) * scale
    gain = lambda k, shape: 1.0 + 0.05 * jax.random.normal(k, shape, f32)
    return {
        "x": jax.random.normal(ks[0], (BATCH, SEQ, D_MODEL), f32),
        "norm_mix_pre": gain(ks[1], (DEPTH, D_MODEL)),
        "norm_mix_post": gain(ks[2], (DEPTH, D_MODEL)),
        "norm_ffn_pre": gain(ks[3], (DEPTH, D_MODEL)),
        "norm_ffn_post": gain(ks[4], (DEPTH, D_MODEL)),
        "w_in": nrm(ks[5], (DEPTH, D_MODEL, D_IN), D_MODEL ** -0.5),
        "conv_a": nrm(ks[6], (DEPTH, CONV_WIDTH, D_CONV), CONV_WIDTH ** -0.5),
        "gate_up_fwd": nrm(ks[7], (DEPTH, GATE_RANK, D_GLA_K), GATE_RANK ** -0.5),
        "gate_bias_fwd": nrm(ks[8], (DEPTH, D_GLA_K), 0.1),
        "gate_up_bwd": nrm(ks[9], (DEPTH, GATE_RANK, D_GLA_K), GATE_RANK ** -0.5),
        "gate_bias_bwd": nrm(ks[10], (DEPTH, D_GLA_K), 0.1),
        "gla_head_norm": gain(ks[11], (DEPTH, HEAD_V)),
        "w_out": nrm(ks[12], (DEPTH, D_MIX, D_MODEL), D_MIX ** -0.5),
        "w_up": nrm(ks[13], (DEPTH, D_MODEL, 2 * D_FF), D_MODEL ** -0.5),
        "conv_ffn": nrm(ks[14], (DEPTH, CONV_WIDTH, 2 * D_FF), CONV_WIDTH ** -0.5),
        "w_down": nrm(ks[15], (DEPTH, D_FF, D_MODEL), D_FF ** -0.5),
    }

def first_block(x, norm_mix_pre, norm_mix_post, norm_ffn_pre, norm_ffn_post, w_in, conv_a,
              gate_up_fwd, gate_bias_fwd, gate_up_bwd, gate_bias_bwd, gla_head_norm,
              w_out, w_up, conv_ffn, w_down):
    for l in range(DEPTH):
        h = rmsnorm(x, norm_mix_pre[l])
        y = mixer(h, w_in[l], conv_a[l], gate_up_fwd[l], gate_bias_fwd[l], gate_up_bwd[l],
                  gate_bias_bwd[l], gla_head_norm[l], w_out[l])
        x = x + rmsnorm(y, norm_mix_post[l])
        h = rmsnorm(x, norm_ffn_pre[l])
        y = conv_mlp(h, w_up[l], conv_ffn[l], w_down[l])
        x = x + rmsnorm(y, norm_ffn_post[l])
    return x


QBLK = 128
P_DIM = 256
MLA_HEADS = 8
Q_LORA = 256
KV_LORA = 128
NOPE_D = 64
ROPE_D = 32
V_D = 64
ROPE_THETA = 10000.0
ML_HEADS = 4
ML_HD = 128
ML_W = ML_HEADS * ML_HD
CONV_K = 4
MIX_W = MLA_HEADS * V_D + ML_W
IN_W = Q_LORA + KV_LORA + ROPE_D + ML_W + ML_W + ML_HEADS + ML_HEADS
N_GROUPS = 4
EXPERTS_PER_GROUP = 8
N_EXPERTS = N_GROUPS * EXPERTS_PER_GROUP
TOP_K = 2
D_EXPERT = 256
MOE_BLK = 128


def _rmsnorm(x, g):
    xf = x.astype(jnp.float32)
    r = lax.rsqrt(jnp.mean(xf * xf, axis=-1, keepdims=True) + EPS)
    return (xf * r * g.astype(jnp.float32)).astype(x.dtype)

def _split_in(proj):
    sizes = (Q_LORA, KV_LORA, ROPE_D, ML_W, ML_W, ML_HEADS, ML_HEADS)
    offs = np.cumsum(sizes)[:-1].tolist()
    return jnp.split(proj, offs, axis=-1)

def _rope_cs(positions):
    inv = 1.0 / (ROPE_THETA ** (jnp.arange(0, ROPE_D, 2, dtype=jnp.float32) / ROPE_D))
    ang = positions.astype(jnp.float32)[..., None] * inv
    return jnp.cos(ang), jnp.sin(ang)

def _apply_rope(x, cos, sin):
    xf = x.astype(jnp.float32)
    x1, x2 = xf[..., :ROPE_D // 2], xf[..., ROPE_D // 2:]
    return jnp.concatenate([x1 * cos - x2 * sin, x1 * sin + x2 * cos], axis=-1).astype(x.dtype)

def _mla_attention(q_nope, q_rope, k_nope, k_rope, v):
    B, S = q_nope.shape[:2]
    nq = S // QBLK
    scale = 1.0 / math.sqrt(NOPE_D + ROPE_D)
    k_chunk = jnp.arange(S) // CHUNK

    def blocks(t):
        return t.reshape(B, nq, QBLK, MLA_HEADS, t.shape[-1]).transpose(1, 0, 3, 2, 4)

    def one(args):
        qn, qr, blk = args
        s = (jnp.einsum('bhqd,bkhd->bhqk', qn, k_nope)
             + jnp.einsum('bhqr,bkr->bhqk', qr, k_rope)).astype(jnp.float32) * scale
        q_chunk = (blk * QBLK + jnp.arange(QBLK)) // CHUNK
        mask = k_chunk[None, :] <= q_chunk[:, None]
        s = jnp.where(mask, s, -1e30)
        pr = jax.nn.softmax(s, axis=-1).astype(v.dtype)
        return jnp.einsum('bhqk,bkhv->bhqv', pr, v)

    o = lax.map(one, (blocks(q_nope), blocks(q_rope), jnp.arange(nq)))
    return o.transpose(1, 0, 3, 2, 4).reshape(B, S, MLA_HEADS * V_D)

def _causal_conv(x, w, b):
    S = x.shape[1]
    xp = jnp.pad(x, ((0, 0), (CONV_K - 1, 0), (0, 0)))
    return sum(xp[:, k:k + S] * w[k] for k in range(CONV_K)) + b

def _mlstm_chunkwise(q, k, v, i_pre, f_pre):
    B, H, S, dk = q.shape
    dv = v.shape[-1]
    L = CHUNK
    nc = S // L

    def chunks(t):
        return t.reshape(B, H, nc, L, t.shape[-1]).transpose(2, 0, 1, 3, 4).astype(jnp.float32)

    qc, kc, vc = chunks(q), chunks(k), chunks(v)
    ic = i_pre.astype(jnp.float32).reshape(B, H, nc, L).transpose(2, 0, 1, 3)
    logf = jax.nn.log_sigmoid(f_pre.astype(jnp.float32)).reshape(B, H, nc, L).transpose(2, 0, 1, 3)
    bc = jnp.cumsum(logf, axis=-1)
    tril = jnp.tril(jnp.ones((L, L), dtype=bool))

    def step(carry, inp):
        C, n, m = carry
        q_, k_, v_, i_, b_ = inp
        D = b_[..., :, None] - b_[..., None, :] + i_[..., None, :]
        D = jnp.where(tril, D, -jnp.inf)
        inter = b_ + m[..., None]
        m_t = jnp.maximum(jnp.max(D, axis=-1), inter)
        w_intra = jnp.exp(D - m_t[..., None])
        w_inter = jnp.exp(inter - m_t)
        qk = jnp.einsum('bhtd,bhsd->bhts', q_, k_) * w_intra
        num = jnp.einsum('bhts,bhsv->bhtv', qk, v_) + w_inter[..., None] * jnp.einsum('bhtd,bhdv->bhtv', q_, C)
        den = jnp.sum(qk, axis=-1) + w_inter * jnp.einsum('bhtd,bhd->bht', q_, n)
        den = jnp.maximum(jnp.abs(den), jnp.exp(-m_t))
        h = num / den[..., None]
        bL = b_[..., -1]
        w_s = bL[..., None] - b_ + i_
        m_new = jnp.maximum(bL + m, jnp.max(w_s, axis=-1))
        ws = jnp.exp(w_s - m_new[..., None])
        decay = jnp.exp(bL + m - m_new)
        C_new = decay[..., None, None] * C + jnp.einsum('bhs,bhsd,bhsv->bhdv', ws, k_, v_)
        n_new = decay[..., None] * n + jnp.einsum('bhs,bhsd->bhd', ws, k_)
        return (C_new, n_new, m_new), h

    init = (jnp.zeros((B, H, dk, dv), jnp.float32), jnp.zeros((B, H, dk), jnp.float32),
            jnp.zeros((B, H), jnp.float32))
    _, hs = lax.scan(step, init, (qc, kc, vc, ic, bc))
    return hs.transpose(1, 2, 0, 3, 4).reshape(B, H, S, dv)

def _hier_moe(h, w_rg, b_rg, w_re, b_re, w_g, w_u, w_d):
    B, S, D = h.shape
    T = B * S
    hf = h.reshape(T, D)
    g_prob = jax.nn.softmax((hf @ w_rg).astype(jnp.float32) + b_rg.astype(jnp.float32), axis=-1)
    g_top, g_idx = lax.top_k(g_prob, 1)
    e_logits = ((hf @ w_re).astype(jnp.float32) + b_re.astype(jnp.float32)).reshape(T, N_GROUPS, EXPERTS_PER_GROUP)
    e_in = jnp.take_along_axis(e_logits, g_idx[:, :, None], axis=1)[:, 0]
    e_top, e_idx = lax.top_k(jax.nn.softmax(e_in, axis=-1), TOP_K)
    wts = g_top * e_top / jnp.sum(e_top, axis=-1, keepdims=True)
    eid = g_idx * EXPERTS_PER_GROUP + e_idx
    M = T * TOP_K
    P = M + N_EXPERTS * MOE_BLK
    nb = P // MOE_BLK
    flat_e = eid.reshape(M).astype(jnp.int32)
    flat_w = wts.reshape(M)
    flat_tok = jnp.repeat(jnp.arange(T, dtype=jnp.int32), TOP_K)
    order = jnp.argsort(flat_e)
    sorted_e = flat_e[order]
    counts = jnp.zeros((N_EXPERTS,), jnp.int32).at[flat_e].add(1)
    starts = jnp.cumsum(counts) - counts
    padded = (counts + MOE_BLK - 1) // MOE_BLK * MOE_BLK
    pad_ends = jnp.cumsum(padded)
    pad_starts = pad_ends - padded
    dest = pad_starts[sorted_e] + (jnp.arange(M, dtype=jnp.int32) - starts[sorted_e])
    row_tok = jnp.full((P,), T, jnp.int32).at[dest].set(flat_tok[order])
    row_w = jnp.zeros((P,), jnp.float32).at[dest].set(flat_w[order])
    block_e = jnp.minimum(jnp.searchsorted(pad_ends, jnp.arange(nb, dtype=jnp.int32) * MOE_BLK, side='right'),
                          N_EXPERTS - 1)
    x_pad = jnp.concatenate([hf, jnp.zeros((1, D), hf.dtype)], axis=0)
    x_rows = x_pad[row_tok].reshape(nb, MOE_BLK, D)

    def expert(args):
        xb, e = args
        return (jax.nn.silu(xb @ w_g[e]) * (xb @ w_u[e])) @ w_d[e]

    y = lax.map(expert, (x_rows, block_e)).reshape(P, D)
    out = jnp.zeros((T + 1, D), jnp.float32).at[row_tok].add(y.astype(jnp.float32) * row_w[:, None])[:T]
    return out.reshape(B, S, D).astype(h.dtype)

def second_inputs(seed: int = 0) -> dict:
    key = jax.random.key(seed)
    ks = jax.random.split(key, 40)
    f32 = jnp.float32

    def nrm(k, shape, fan_in):
        return jax.random.normal(k, shape, f32) * (fan_in ** -0.5)

    def gain(k, shape):
        return 1.0 + 0.05 * jax.random.normal(k, shape, f32)

    x = jax.random.normal(ks[0], (BATCH, SEQ, D_MODEL), f32)
    p = jax.random.normal(ks[1], (DEPTH, BATCH, SEQ, P_DIM), f32)
    positions = (jax.random.randint(ks[2], (BATCH, 1), 0, 4096, dtype=jnp.int32)
                 + jnp.arange(SEQ, dtype=jnp.int32)[None, :])
    return {
        'x': x,
        'p': p,
        'positions': positions,
        'norm_mix_g': gain(ks[3], (DEPTH, D_MODEL)),
        'w_in': nrm(ks[4], (DEPTH, D_MODEL, IN_W), D_MODEL),
        'q_norm_g': gain(ks[5], (DEPTH, Q_LORA)),
        'w_uq': nrm(ks[6], (DEPTH, Q_LORA, MLA_HEADS * (NOPE_D + ROPE_D)), Q_LORA),
        'kv_norm_g': gain(ks[7], (DEPTH, KV_LORA)),
        'w_ukv': nrm(ks[8], (DEPTH, KV_LORA, MLA_HEADS * (NOPE_D + V_D)), KV_LORA),
        'conv_w': nrm(ks[9], (DEPTH, CONV_K, ML_W), CONV_K),
        'conv_b': 0.02 * jax.random.normal(ks[10], (DEPTH, ML_W), f32),
        'w_mq': nrm(ks[11], (DEPTH, ML_HEADS, ML_HD, ML_HD), ML_HD),
        'w_mk': nrm(ks[12], (DEPTH, ML_HEADS, ML_HD, ML_HD), ML_HD),
        'w_mv': nrm(ks[13], (DEPTH, ML_HEADS, ML_HD, ML_HD), ML_HD),
        'b_igate': 0.1 * jax.random.normal(ks[14], (DEPTH, ML_HEADS), f32),
        'b_fgate': jnp.linspace(3.0, 6.0, ML_HEADS, dtype=f32)[None, :] + 0.1 * jax.random.normal(ks[15], (DEPTH, ML_HEADS), f32),
        'mh_norm_g': gain(ks[16], (DEPTH, ML_W)),
        'ml_skip': gain(ks[17], (DEPTH, ML_W)),
        'w_o': nrm(ks[18], (DEPTH, MIX_W, D_MODEL), MIX_W),
        'norm_ffn_g': gain(ks[19], (DEPTH, D_MODEL)),
        'w_router_group': nrm(ks[20], (DEPTH, D_MODEL, N_GROUPS), D_MODEL),
        'b_router_group': 0.01 * jax.random.normal(ks[21], (DEPTH, N_GROUPS), f32),
        'w_router_expert': nrm(ks[22], (DEPTH, D_MODEL, N_EXPERTS), D_MODEL),
        'b_router_expert': 0.01 * jax.random.normal(ks[23], (DEPTH, N_EXPERTS), f32),
        'w_gate_e': nrm(ks[24], (DEPTH, N_EXPERTS, D_MODEL, D_EXPERT), D_MODEL),
        'w_up_e': nrm(ks[25], (DEPTH, N_EXPERTS, D_MODEL, D_EXPERT), D_MODEL),
        'w_down_e': nrm(ks[26], (DEPTH, N_EXPERTS, D_EXPERT, D_MODEL), D_EXPERT),
        'norm_ple_g': gain(ks[27], (DEPTH, D_MODEL)),
        'w_ple': nrm(ks[28], (DEPTH, P_DIM, D_MODEL), P_DIM),
        'w_ple_gate': nrm(ks[29], (DEPTH, D_MODEL, D_MODEL), D_MODEL),
        'final_norm_g': gain(ks[30], (D_MODEL,)),
    }

def second_block(x, p, positions, norm_mix_g, w_in, q_norm_g, w_uq, kv_norm_g, w_ukv, conv_w, conv_b,
              w_mq, w_mk, w_mv, b_igate, b_fgate, mh_norm_g, ml_skip, w_o, norm_ffn_g,
              w_router_group, b_router_group, w_router_expert, b_router_expert,
              w_gate_e, w_up_e, w_down_e, norm_ple_g, w_ple, w_ple_gate, final_norm_g):
    B, S, _ = x.shape
    cos, sin = _rope_cs(positions)
    for i in range(DEPTH):
        h = _rmsnorm(x, norm_mix_g[i])
        c_q, c_kv, k_r, x_m, z, i_pre, f_pre = _split_in(h @ w_in[i])
        q = (_rmsnorm(c_q, q_norm_g[i]) @ w_uq[i]).reshape(B, S, MLA_HEADS, NOPE_D + ROPE_D)
        kv = (_rmsnorm(c_kv, kv_norm_g[i]) @ w_ukv[i]).reshape(B, S, MLA_HEADS, NOPE_D + V_D)
        q_nope, q_rope = q[..., :NOPE_D], _apply_rope(q[..., NOPE_D:], cos[:, :, None], sin[:, :, None])
        k_nope, v = kv[..., :NOPE_D], kv[..., NOPE_D:]
        k_rope = _apply_rope(k_r, cos, sin)
        attn_out = _mla_attention(q_nope, q_rope, k_nope, k_rope, v)
        xc = jax.nn.silu(_causal_conv(x_m, conv_w[i], conv_b[i]))
        xch = xc.reshape(B, S, ML_HEADS, ML_HD)
        xmh = x_m.reshape(B, S, ML_HEADS, ML_HD)
        mq = jnp.einsum('bshd,hde->bhse', xch, w_mq[i])
        mk = jnp.einsum('bshd,hde->bhse', xch, w_mk[i]) * (ML_HD ** -0.5)
        mv = jnp.einsum('bshd,hde->bhse', xmh, w_mv[i])
        ig = (i_pre + b_igate[i]).transpose(0, 2, 1)
        fg = (f_pre + b_fgate[i]).transpose(0, 2, 1)
        hm = _mlstm_chunkwise(mq, mk, mv, ig, fg).transpose(0, 2, 1, 3)
        mu = jnp.mean(hm, axis=-1, keepdims=True)
        var = jnp.mean(jnp.square(hm - mu), axis=-1, keepdims=True)
        hm = ((hm - mu) * lax.rsqrt(var + EPS)).reshape(B, S, ML_W) * mh_norm_g[i].astype(jnp.float32)
        ml_out = ((hm.astype(x.dtype) + ml_skip[i] * xc) * jax.nn.silu(z)).astype(x.dtype)
        x = x + jnp.concatenate([attn_out, ml_out], axis=-1) @ w_o[i]
        x = x + _hier_moe(_rmsnorm(x, norm_ffn_g[i]), w_router_group[i], b_router_group[i],
                          w_router_expert[i], b_router_expert[i], w_gate_e[i], w_up_e[i], w_down_e[i])
        hp = _rmsnorm(x, norm_ple_g[i])
        x = x + (p[i] @ w_ple[i]) * jax.nn.sigmoid(hp @ w_ple_gate[i])
    return _rmsnorm(x, final_norm_g)


def setup_inputs(seed=0):
    out = dict(first_inputs(seed))
    for name, value in second_inputs(seed + 1).items():
        if name != "x":
            out[name + "_2"] = value
    return out


def reference(
    x, norm_mix_pre, norm_mix_post, norm_ffn_pre, norm_ffn_post, w_in, conv_a, gate_up_fwd,
    gate_bias_fwd, gate_up_bwd, gate_bias_bwd, gla_head_norm, w_out, w_up, conv_ffn, w_down,
    p_2, positions_2, norm_mix_g_2, w_in_2, q_norm_g_2, w_uq_2, kv_norm_g_2, w_ukv_2, conv_w_2,
    conv_b_2, w_mq_2, w_mk_2, w_mv_2, b_igate_2, b_fgate_2, mh_norm_g_2, ml_skip_2, w_o_2,
    norm_ffn_g_2, w_router_group_2, b_router_group_2, w_router_expert_2, b_router_expert_2,
    w_gate_e_2, w_up_e_2, w_down_e_2, norm_ple_g_2, w_ple_2, w_ple_gate_2, final_norm_g_2,
):
    x = first_block(
        x, norm_mix_pre, norm_mix_post, norm_ffn_pre, norm_ffn_post, w_in, conv_a, gate_up_fwd,
        gate_bias_fwd, gate_up_bwd, gate_bias_bwd, gla_head_norm, w_out, w_up, conv_ffn, w_down,
    )
    return second_block(
        x, p_2, positions_2, norm_mix_g_2, w_in_2, q_norm_g_2, w_uq_2, kv_norm_g_2, w_ukv_2,
        conv_w_2, conv_b_2, w_mq_2, w_mk_2, w_mv_2, b_igate_2, b_fgate_2, mh_norm_g_2,
        ml_skip_2, w_o_2, norm_ffn_g_2, w_router_group_2, b_router_group_2, w_router_expert_2,
        b_router_expert_2, w_gate_e_2, w_up_e_2, w_down_e_2, norm_ple_g_2, w_ple_2,
        w_ple_gate_2, final_norm_g_2,
    )


_drawn_inputs = setup_inputs


def setup_inputs(seed=0):
    import zlib

    import numpy as np

    out = dict(_drawn_inputs(seed))
    spreads = {}
    factors = {'gate_bias_fwd': 2.871,
     'gate_bias_bwd': 2.804,
     'q_norm_g_2': 8.0,
     'kv_norm_g_2': 7.984,
     'conv_b_2': 3.882,
     'b_igate_2': 64.0,
     'mh_norm_g_2': 13.791,
     'ml_skip_2': 24.863,
     'b_router_group_2': 64.0,
     'b_router_expert_2': 42.057,
     'norm_ple_g_2': 64.0,
     'norm_ffn_g_2': 6.189}
    for name, (base, spread) in spreads.items():
        noise = np.random.default_rng([zlib.crc32(name.encode()), seed]).standard_normal(out[name].shape)
        drawn = base * np.exp(spread * noise) if base else spread * noise
        out[name] = jnp.asarray(drawn.astype(out[name].dtype))
    for name, factor in factors.items():
        out[name] = (out[name] * factor).astype(out[name].dtype)
    return out
```

```python
from contextlib import ExitStack

import numpy as np
import concourse.bass as bass
from concourse import mybir

F32 = mybir.dt.float32
F32R = mybir.dt.float32r
BF16 = mybir.dt.bfloat16
I32 = mybir.dt.int32
ALU = mybir.AluOpType
ACT = mybir.ActivationFunctionType
AX = mybir.AxisListType.X

P = 128
SEQ = 256
TB = SEQ // P
D = 1024
KD = D // P
EPS = 1e-6
NEG = -1e30

HEADS = 4
CH = 64
NCH = SEQ // CH
RANK = 16
D_FF = 2816
NT = D_FF // P
NPAIR = NT // 2
C_GB, C_GC, C_GV, C_Q, C_K, C_V, C_GO, C_LR = 0, 512, 1024, 1536, 1792, 2048, 2560, 3072
A_HEADS = 8
NOPE, ROPE, VD = 64, 32, 64
QL, KVL = 256, 128
HQ = NOPE + ROPE
A_SCALE = 1.0 / float(np.sqrt(NOPE + ROPE))
THETA = 10000.0
M_HEADS = 4
C2_KR, C2_XM, C2_Z, C2_I = QL + KVL, QL + KVL + ROPE, QL + KVL + ROPE + 512, QL + KVL + ROPE + 1024
N_EXP, N_GRP, EPG, F_EXP = 32, 4, 8, 256
NEP = N_EXP // 2
CAP = 64
UNIT = 4096
SLOTS = 6


ROWS = (("norm_mix_pre", 8), ("norm_ffn_pre", 8), ("conv_a", 12), ("gate_bias_fwd", 2), ("gate_bias_bwd", 2),
        ("gla_head_norm", 1), ("norm_mix_g_2", 8), ("q_norm_g_2", 2), ("kv_norm_g_2", 1), ("conv_w_2", 16),
        ("conv_b_2", 4), ("mh_norm_g_2", 4), ("ml_skip_2", 4), ("norm_ffn_g_2", 8), ("norm_ple_g_2", 8))


def build(nc, a, out):
    with ExitStack() as ctx:
        sems = {}

        STEPS = {
            "pe_mix1": (("lr_done", 1), ("q_done", 1), ("pre_done", 2), ("k_done", 1), ("v_done", 2), ("gc_done", 2),
                        ("gv_done", 2), ("gb_done", 2), ("go_done", 2), ("scores_done", 4), ("kot_done", 2),
                        ("kv_done", 3), ("o_done", 2), ("onT_done", 2)),
            "pe_mix2": (("icol_done", 1), ("c_done", 2), ("if_done", 1), ("kr_done", 1), ("xm_done", 2), ("cT_done", 2),
                        ("z2_done", 2), ("qa_done", 4), ("ka_done", 4), ("v2_done", 2), ("gT_done", 1), ("negM_done", 2),
                        ("mq_done", 2), ("mk_done", 2), ("mv_done", 2)),
            "pe_route": (("hmT_done", 2), ("y2_done", 2), ("logits_done", 1), ("pT_done", 1), ("rank_done", 1)),
            "act_mix1": (("lr_ready", 1), ("q_ready", 1), ("ln_ready", 1), ("k_ready", 1), ("v_ready", 2),
                         ("exp_ready", 4), ("gc_ready", 2), ("gb_ready", 2), ("sgo_ready", 2), ("kot_ready", 2),
                         ("osq_ready", 1), ("ostd_ready", 1)),
            "act_mix2": (("cstd_ready", 1), ("gln_ready", 1), ("cs_ready", 2), ("xm_ready", 2), ("sz_ready", 2),
                         ("xc_ready", 4), ("qn_ready", 4), ("kn_ready", 4), ("v2_ready", 2), ("floor_ready", 1),
                         ("mq_ready", 2), ("mk_ready", 2), ("mv_ready", 2), ("wexp_ready", 4)),
            "dve_mix1": (("z_ready", 2), ("rest_half", 1), ("cum_ready", 1), ("qk_ready", 6), ("m_ready", 2),
                         ("conv_a", 9), ("ya_ready", 1), ("PT_ready", 4), ("oms_ready", 1), ("on_ready", 2),
                         ("yb_ready", 2)),
            "dve_mix2": (("icol_ready", 1), ("cn_ready", 4), ("gz_ready", 2), ("cT_ready", 2), ("gates_ready", 1),
                         ("conv2_done", 4), ("kr_ready", 1), ("qr_ready", 4), ("ucol_ready", 1)),
            "dve_route": (("hmn_ready", 8), ("ym_ready", 2), ("rt_clear", 2), ("pT_ready", 1), ("gsub_ready", 1),
                          ("msub_ready", 1), ("sel_ready", 1)),
        }
        shared = {}
        for group, steps in STEPS.items():
            base = 0
            for step, count in steps:
                shared[step] = (group, base)
                base += count

        def at(name, n):
            return n + shared[name][1] if name in shared else n

        def sig(name):
            name = shared[name][0] if name in shared else name
            if name not in sems:
                sems[name] = ctx.enter_context(nc.semaphore(name))
            return sems[name]

        def sb(name, shape, dt=F32):
            return ctx.enter_context(nc.sbuf_tensor(name, shape, dt))

        ps = ctx.enter_context(nc.psum_tensor("ps", [P, 8, 512], F32))

        x_tok = sb("x_tok", [P, TB, D])
        hn = sb("hn", [P, TB, D])
        hT = sb("hT", [P, KD, SEQ])
        W_at = nc.sbuf_base
        W = sb("W", [P, SLOTS * UNIT])
        junk = sb("junk", [P, D])
        gbc = sb("gbc", [P, D])
        ident = sb("ident", [P, P])
        ones = sb("ones", [P, P])
        zb = sb("zb", [P, 512], BF16)
        mask2 = sb("mask2", [P, 2, P])
        epsc = sb("epsc", [P, 1])
        prow = sb("prow", [P, P])
        par = sb("par", [P, P])
        stat = sb("stat", [P, 64])
        small = sb("small", [P, 48])
        cw = sb("cw", [P, 132])[:]
        NAR = 18688
        arena_at = nc.sbuf_base
        arena = sb("arena", [P, NAR])

        def split_pair(name, base, word, n):
            return [nc.alloc_sbuf_tensor_at(f"{name}_{part}", [P, n], F32R, offset=base + 4 * (word + k * n)).ap()
                    for k, part in enumerate(("high", "low"))]

        def slot(n):
            s = (n % SLOTS) * UNIT
            return W[:, s:s + UNIT]

        col = {}
        NROW = 0
        for name, n in ROWS:
            col[name] = NROW
            NROW += n

        off = [0]

        def take(n):
            o = off[0]
            off[0] += n
            assert off[0] <= NAR, off
            return arena[:, o:o + n]

        def v3(t, a_):
            return t.rearrange("p (a b) -> p a b", a=a_)

        def v4(t, a_, b_):
            return t.rearrange("p (a b c) -> p a b c", a=a_, b=b_)

        yT = hT
        gbT = v3(take(1024), 4)
        mT = v3(take(4 * 258), 4)
        gcT = v3(take(1024), 4)
        cv = gcT
        qT = take(512)
        kT = take(512)
        v_tok = v3(take(1024), TB)
        sgo = v3(take(1024), 4)
        zz = v3(take(1024), 2)
        t1 = v3(take(1024), 2)
        la = v3(take(1024), 2)
        cum = v3(take(1024), 2)
        E1, E2 = t1, zz
        tmp = v3(take(1024), 2)
        q_in = v3(take(1024), 2)
        k_in = v3(take(1024), 2)
        k_out = v3(take(1024), 2)
        on = tmp
        tmpP = v4(take(512), 2, 2)
        S_st = v4(take(6 * 256), 6, 2)
        tot = v3(take(16), 2)
        dec = v3(take(16), 2)
        wlr = v3(take(256), KD)
        lr = v3(take(512), 2)
        gup = v3(take(512), 2)
        rmask = take(512)
        kot = hn[:, 0, :].rearrange("p (b d j c) -> p b d j c", b=2, d=2, j=2)
        PT = hn[:, 1, :].rearrange("p (b h i) -> p b h i", b=2, h=4)
        off[0] = 0
        uact = [v3(take(512), 2) for _ in range(2)]
        gact = [v3(take(512), 2) for _ in range(2)]
        cgt = [v3(take(512), 2) for _ in range(2)]
        cvt = [v3(take(512), 2) for _ in range(2)]

        cwp = [take(12) for _ in range(2)]
        frow3 = hn[0:44, 0, 0:3 * P].rearrange("r (t c) -> r t c", t=3)

        assert off[0] <= 4224
        off[0] = 4224
        sel4 = v3(take(512), 4)
        cmask = take(256)
        amask = take(256)
        wif = v3(take(64), KD)
        wr = v3(take(288), KD)
        brt = take(36)
        bif = take(2)
        invrow = take(32)
        sgn = take(1)
        icol = take(1)
        iot = take(64)
        ustrict = take(P)
        onesr = take(256)
        posi = onesr
        ptok = v3(take(512), 2)
        off[0] += -(arena_at // 4 + off[0]) % 8
        KEEP = off[0]
        w_up_hl = [v4(t, 4, KD) for t in split_pair("w_up", arena_at, KEEP, 4096)]
        uact_hl = [v4(t, 2, 2) for t in split_pair("uact", arena_at, KEEP + 8192, 1024)]
        hT_hl = [v3(t, KD) for t in split_pair("hT", W_at, 0, 2048)]
        w_dn_hl = [v3(t, 2) for t in split_pair("w_down", W_at, UNIT, 2048)]
        assert KEEP + 8192 + 2048 <= NAR
        cosT = take(256)
        sinT = take(256)
        region = take(1536)
        krw = v3(region[:, 0:256], KD)
        uqw = region[:, 256:768].rearrange("p (k h c) -> p k h c", k=2, h=A_HEADS)
        cn = v3(region[:, 768:1536], 2)
        wexp = v3(region, 4)
        cT = v3(take(768), 3)
        xmT = v3(take(4 * 259), 4)
        szT = v3(take(1024), 4)
        xcT = v3(take(1024), 4)
        mqT = v3(take(1024), 4)
        mkT = v3(take(1024), 4)
        vext = take(2 * 4 * 129).rearrange("p (b h e) -> p b h e", b=2, h=4)
        kTa = v3(take(2048), A_HEADS)
        hmt = v3(take(1024), 2)
        assert off[0] <= NAR
        off[0] = 0
        qTa = v3(take(2048), A_HEADS)
        v2 = v3(take(1024), 2)
        bns = v3(take(48), 8)
        gat = v3(take(6 * 128 + 256), 4)
        assert off[0] <= 4224
        sP = [v3(hn[:, 0, 512 * q:512 * q + 512], 2) for q in range(2)]
        PTs = [v3(hn[:, 1, 512 * q:512 * q + 512], 4) for q in range(2)]
        pm = [junk[:, 384 * q:384 * q + 384] for q in range(2)]
        ucol = stat[:, 52:60]
        ufl = small[:, 0:8]
        amx = [small[:, 8 + 2 * q:10 + 2 * q] for q in range(2)]
        asum = [small[:, 12 + 2 * q:14 + 2 * q] for q in range(2)]
        hden = small[:, 16:18]
        mmv = v3(small[:, 18:34], 8)
        mstd = small[:, 34:42]
        ang, angr = hmt[:, 0, 0:256], hmt[:, 0, 256:512]
        rtb = [hmt[:, 1, 0:512], hmt[:, 0, 0:512]]
        off[0] = 0
        OH = [v3(take(256), 2) for _ in range(2)]
        OHW = [v3(take(256), 2) for _ in range(2)]
        SC = [take(256) for _ in range(2)]
        aT = [v3(take(256), 2) for _ in range(2)]
        sg = [take(256) for _ in range(2)]
        atok = [take(256) for _ in range(2)]
        rkp = [take(4) for _ in range(2)]
        wkp = [take(4) for _ in range(2)]
        off[0] = KEEP
        xg = [v3(take(1024), KD) for _ in range(2)]
        Yp = [v3(take(1024), 2) for _ in range(2)]
        RK = take(64)
        WK = take(64)
        Lg = v3(take(72), 2)
        e32 = [v3(take(64), 2) for _ in range(6)]
        g4 = [v3(take(8), 2) for _ in range(4)]
        sm = [take(2) for _ in range(12)]
        nrf = take(8)
        nri = nrf[:, 4:5].bitcast(I32)
        pT = v3(take(512), 2)
        sgate = v3(take(2048), 2)
        assert off[0] <= NAR, off

        def par_c(name, i, n=1):
            c = col[name] + i
            return par[:, c:c + n]

        w_in = a["w_in"][0].rearrange("(k p) n -> p k n", p=P)
        w_out = a["w_out"][0].rearrange("(k p) n -> p k n", p=P)
        w_up = a["w_up"][0].rearrange("(k p) n -> p k n", p=P)
        w_down = a["w_down"][0].rearrange("(k p) n -> p k n", p=P)

        dense = [(w_in[:, :, c:c + 512], 512) for c in (C_Q, C_V, C_GC, C_GV, C_GB, C_GO)]
        dense += [(w_out[:, :, c:c + 512], 512) for c in (0, 512)]
        N_D1 = len(dense)
        w_in2 = a["w_in_2"][0].rearrange("(k p) n -> p k n", p=P)
        w_o = a["w_o_2"][0].rearrange("(k p) n -> p k n", p=P)
        w_pg = a["w_ple_gate_2"][0].rearrange("(k p) n -> p k n", p=P)
        wA = W[:, 5 * UNIT:6 * UNIT][:, 0:KD * 416].rearrange("p (k n) -> p k n", k=KD)
        PAN = [W[:, s * UNIT:(s + 1) * UNIT].rearrange("p (k n) -> p k n", k=KD) for s in range(SLOTS)]
        uq = W[:, 2 * UNIT:2 * UNIT + 1536].rearrange("p (k n) -> p k n", k=2)
        ukv = W[:, 2 * UNIT + 1536:2 * UNIT + 2560]
        wm = W[:, 3 * UNIT:3 * UNIT + 1536].rearrange("p (m h e) -> p m h e", m=3, h=M_HEADS)
        wple = W[:, 2 * UNIT:2 * UNIT + 2048].rearrange("p (k n) -> p k n", k=2)
        GU = [[W[:, (3 * q + e) * UNIT:(3 * q + e + 1) * UNIT].rearrange("p (k g n) -> p k g n", k=KD, g=2)
               for e in range(2)] for q in range(2)]
        DE = [W[:, (3 * q + 2) * UNIT:(3 * q + 3) * UNIT].rearrange("p (e f n) -> p e f n", e=2, f=2) for q in range(2)]
        w_ge = a["w_gate_e_2"][0].rearrange("e (k p) n -> p e k n", p=P)
        w_ue = a["w_up_e_2"][0].rearrange("e (k p) n -> p e k n", p=P)
        w_de = a["w_down_e_2"][0].rearrange("e (f p) n -> p e f n", p=P)

        def panel(n, width=512):
            return slot(n)[:, 0:KD * width].rearrange("p (k n) -> p k n", k=KD)

        U = [W[:, s * UNIT:(s + 1) * UNIT].rearrange("p (k g n) -> p k g n", k=KD, g=2) for s in (2, 3)]
        DN = [W[:, 4 * UNIT + s * 2048:4 * UNIT + (s + 1) * 2048].rearrange("p (i n) -> p i n", i=2) for s in (0, 1)]

        KV_AT = (((3, 0), (1, 0), (3, 256)), ((0, 0), (4, 0), (0, 256)))

        def o_ps(b):
            return ps[:, 6:8, 256 * b:256 * b + 256].rearrange("p h (j c) -> p h j c", j=2)

        block = ctx.enter_context(nc.Block())

        @block.sync
        def _(sp):
            for b in range(TB):
                sp.dma_start(x_tok[:, b, :], a["x"][0, b * P:(b + 1) * P, :]).then_inc(sig("x_landed"), 16)
            sp.dma_start(wlr, w_in[:, :, C_LR:C_LR + 32], ).then_inc(sig("wlr_landed"), 16)
            for n, (src, width) in enumerate(dense):
                if n == 1:
                    sp.wait_ge(sig("frow_landed"), 16)
                if n >= SLOTS:
                    sp.wait_ge(sig("panel_used"), n - SLOTS + 1)
                sp.dma_start(panel(n, width), src).then_inc(sig(f"landed{n % SLOTS}"), 16)
                if n == 0:
                    for i, name in enumerate(("gate_up_fwd", "gate_up_bwd")):
                        sp.dma_start(gup[0:RANK, i, :], a[name][0]).then_inc(sig("gup_landed"), 16)
            sp.wait_ge(sig("panel_used"), 5)

            def load_up(i, s):
                for g in range(2):
                    sp.dma_start(U[s][:, :, g, :],
                                 w_up[:, :, bass.ds(i * 256 + g * D_FF, 256)]).then_inc(sig(f"up_landed{s}"), 16)

            def load_down(i, s):
                sp.dma_start(DN[s], w_down[:, bass.ds(i * 2, 2), :]).then_inc(sig(f"down_landed{s}"), 16)

            load_up(0, 0)
            load_down(0, 0)
            load_up(1, 1)
            load_down(1, 1)

            def reload(i, q):
                sp.wait_ge(sig("up_low"), i * 8 + 4 * q + 4)
                load_up(i * 2 + q + 2, q)
                sp.wait_ge(sig("down_low"), i * 4 + 2 * q + 2)
                load_down(i * 2 + q + 2, q)

            sp.wait_ge(sig("panel_used"), N_D1)
            sp.dma_start(wA, w_in2[:, :, 0:416]).then_inc(sig("a2_landed"), 16)
            sp.wait_ge(sig("x_ready"), 2)
            for dst, src in ((wif, w_in2[:, :, C2_I:C2_I + 8]),
                             (wr[:, :, 0:N_GRP], a["w_router_group_2"][0].rearrange("(k p) n -> p k n", p=P)),
                             (wr[:, :, N_GRP:36], a["w_router_expert_2"][0].rearrange("(k p) n -> p k n", p=P)),
                             (brt[:, 0:N_GRP], a["b_router_group_2"][0:1, :].broadcast_to([P, N_GRP])),
                             (brt[:, N_GRP:36], a["b_router_expert_2"][0:1, :].broadcast_to([P, N_EXP])),
                             (bif[0:4, 0:1], a["b_igate_2"][0:1, :].rearrange("a h -> h a")),
                             (bif[0:4, 1:2], a["b_fgate_2"][0:1, :].rearrange("a h -> h a")),
                             (posi[64:96, :].bitcast(I32), a["positions_2"][0:1, :].broadcast_to([ROPE, SEQ])),
                             (ptok, a["p_2"][0, 0].rearrange("(b p) c -> p b c", p=P))):
                sp.dma_start(dst, src).then_inc(sig("small_landed"), 16)

            with sp.Fori(0, NPAIR // 2 - 1) as i:
                reload(i, 0)
                reload(i, 1)
            reload(NPAIR // 2 - 1, 0)

            sp.wait_ge(sig("mlp_done"), 1)
            sp.dma_start(PAN[0], w_in2[:, :, C2_XM:C2_XM + 512]).then_inc(sig("xm_landed"), 16)
            sp.dma_start(PAN[1], w_in2[:, :, C2_Z:C2_Z + 512]).then_inc(sig("zw_landed"), 16)
            sp.dma_start(uq, a["w_uq_2"][0].rearrange("(k p) n -> p k n", p=P)).then_inc(sig("uq_landed"), 16)
            sp.dma_start(ukv, a["w_ukv_2"][0]).then_inc(sig("uq_landed"), 16)
            sp.dma_start(wm[:, 0], a["w_mq_2"][0].rearrange("h d e -> d h e")).then_inc(sig("wm_landed"), 16)
            sp.dma_start(wm[:, 1], a["w_mk_2"][0].rearrange("h d e -> d h e")).then_inc(sig("wm_landed"), 16)
            sp.dma_start(wm[:, 2], a["w_mv_2"][0].rearrange("h d e -> d h e")).then_inc(sig("wm_landed"), 16)
            sp.dma_start(PAN[4], w_o[:, :, 0:512]).then_inc(sig("wo0_landed"), 16)
            sp.wait_ge(sig("a2_used"), 1)
            sp.dma_start(PAN[5], w_o[:, :, 512:1024]).then_inc(sig("wo1_landed"), 16)

            def load_gu(expert, q, e):
                for g, w in ((0, w_ge), (1, w_ue)):
                    sp.dma_start(GU[q][e][:, :, g, :], w[:, bass.ds(expert, 1), :, :].rearrange("p e k n -> p (e k) n"))\
                      .then_inc(sig(f"gu{e}_landed{q}"), 16)

            def load_de(expert, q):
                sp.dma_start(DE[q], w_de[:, bass.ds(expert, 2), :, :]).then_inc(sig(f"de_landed{q}"), 16)

            sp.wait_ge(sig("xm_used"), 1)
            load_gu(0, 0, 0)
            sp.wait_ge(sig("zw_used"), 1)
            load_gu(1, 0, 1)
            sp.wait_ge(sig("uq_used"), 1)
            load_de(0, 0)
            sp.wait_ge(sig("wm_used"), 1)
            load_gu(2, 1, 0)
            sp.wait_ge(sig("wo_used"), 1)
            load_gu(3, 1, 1)
            load_de(2, 1)
            sp.wait_ge(sig("rounds_ready"), 1)
            rounds = sp.value_load(nri[0:1, :], min_val=1, max_val=SEQ // CAP)

            def reload_pair(h, t, q):
                first, second, turn = t * 2, t * 2 + 1, h + 1
                if not isinstance(t, int):
                    first, second = sp.snap(first), sp.snap(second)
                turn = sp.snap(turn)
                for e in range(2):
                    sp.wait_ge(sig(f"gu{e}_used{q}"), turn)
                    load_gu((first, second)[e], q, e)
                sp.wait_ge(sig(f"de_used{q}"), turn)
                load_de(first, q)

            with sp.Fori(0, rounds) as r:
                with sp.Fori(0, NEP // 2 - 1) as i:
                    for q in range(2):
                        reload_pair(r * (NEP // 2) + i, i * 2 + 2 + q, q)
                for q in range(2):
                    reload_pair(r * (NEP // 2) + NEP // 2 - 1, q, q)

            sp.wait_ge(sig("slots_free"), 1)
            sp.dma_start(wple, a["w_ple_2"][0].rearrange("(k p) n -> p k n", p=P)).then_inc(sig("wple_landed"), 16)
            sp.dma_start(PAN[3], w_pg[:, :, 0:512]).then_inc(sig("pg0_landed"), 16)
            sp.dma_start(PAN[4], w_pg[:, :, 512:1024]).then_inc(sig("pg1_landed"), 16)
            for b in range(TB):
                sp.wait_ge(sig("out_ready"), b + 1)
                sp.dma_start(out[0, b * P:(b + 1) * P, :], hn[:, b, :]).then_inc(sig("stored"), 16)
            sp.wait_ge(sig("stored"), 32)

        @block.gpsimd
        def _(pool):
            pool.memset(ident[:], 0.0).then_inc(sig("cleared"), 1)
            pool.memset(ones[:], 1.0).then_inc(sig("cleared"), 1)
            pool.memset(mask2[:], 1.0).then_inc(sig("cleared"), 1)
            pool.memset(epsc[:], EPS).then_inc(sig("cleared"), 1)
            pool.memset(zb[:], 0.0).then_inc(sig("cleared"), 1)
            pool.memset(rmask, 1.0).then_inc(sig("cleared"), 1)
            pool.memset(mT[:, :, 0:1], 0.0).then_inc(sig("cleared"), 1)
            pool.memset(mT[:, :, 257:258], 0.0).then_inc(sig("cleared"), 1)
            pool.wait_ge(sig("cleared"), 8)
            pool.affine_select(out=ident[:], in_=ident[:], compare_op=ALU.not_equal, fill=1.0, base=0,
                               pattern=[[-1, P]], channel_multiplier=1).then_inc(sig("ident_ready"), 1)
            pool.memset(rmask.rearrange("p (c t) -> p c t", t=CH)[:, :, 0:1], 0.0).then_inc(sig("rmask_ready"), 1)
            pool.affine_select(out=mask2[:, 0, :], in_=mask2[:, 0, :], compare_op=ALU.is_ge, fill=0.0, base=0,
                               pattern=[[1, P]], channel_multiplier=-1).then_inc(sig("mask_cut"), 1)
            pool.affine_select(out=mask2[:, 1, :], in_=mask2[:, 1, :], compare_op=ALU.is_ge, fill=0.0, base=0,
                               pattern=[[-1, P]], channel_multiplier=1).then_inc(sig("mask_cut"), 1)
            pool.wait_ge(sig("mask_cut"), 2)
            pool.affine_select(out=mask2[:, :, 0:CH], in_=mask2[:, :, 0:CH], compare_op=ALU.is_ge, fill=0.0,
                               base=CH - 1, pattern=[[0, 2], [0, CH]], channel_multiplier=-1).then_inc(sig("mask_cut"), 1)
            pool.affine_select(out=mask2[:, :, CH:P], in_=mask2[:, :, CH:P], compare_op=ALU.is_ge, fill=0.0,
                               base=-CH, pattern=[[0, 2], [0, CH]], channel_multiplier=1).then_inc(sig("mask_cut"), 1)

            pool.wait_ge(sig("x_ready"), 2)
            n = 0
            for t, v in ((sel4, 0.0), (cmask, 0.0), (amask, 0.0), (sgn[64:96, :], 1.0), (ustrict, 1.0), (onesr[0:4], 1.0)):
                pool.memset(t, v).then_inc(sig("cleared2"), 1)
                n += 1
                pool.wait_ge(sig("cleared2"), n)
            for i in range(ROPE // 2):
                inv = float(np.float32(1.0) / np.float32(np.float32(THETA) ** (np.float32(2 * i) / np.float32(ROPE))))
                pool.memset(invrow[0:1, i:ROPE:ROPE // 2], inv).then_inc(sig("cleared2"), 1)
                n += 1
                pool.wait_ge(sig("cleared2"), n)
            pool.iota(iot, pattern=[[1, 64]], base=0, channel_multiplier=0,
                      allow_small_or_imprecise_dtypes=True).then_inc(sig("cleared2"), 1)
            pool.wait_ge(sig("cleared2"), n + 1)
            pool.affine_select(out=sel4[0:4], in_=sel4[0:4], compare_op=ALU.not_equal, fill=-1.0, base=0,
                               pattern=[[-1, 4], [0, P]], channel_multiplier=1).then_inc(sig("const2"), 1)
            pool.wait_ge(sig("const2"), 1)
            pool.affine_select(out=cmask[:, 0:P], in_=cmask[:, 0:P], compare_op=ALU.is_ge, fill=NEG, base=0,
                               pattern=[[1, P]], channel_multiplier=-1).then_inc(sig("const2"), 1)
            pool.wait_ge(sig("const2"), 2)
            pool.affine_select(out=ustrict, in_=ustrict, compare_op=ALU.is_gt, fill=0.0, base=0,
                               pattern=[[1, P]], channel_multiplier=-1).then_inc(sig("const2"), 1)
            pool.wait_ge(sig("const2"), 3)
            pool.memset(amask[0:64, P + CH:2 * P], NEG).then_inc(sig("const2"), 1)
            pool.wait_ge(sig("const2"), 4)
            pool.memset(sgn[64:80, :], -1.0).then_inc(sig("const2"), 1)
            pool.wait_ge(sig("const2"), 5)
            pool.wait_ge(sig("mlp_done"), 1)
            pool.memset(xmT[:, :, 0:3], 0.0).then_inc(sig("edges_ready"), 1)
            pool.wait_ge(sig("edges_ready"), 1)
            pool.memset(vext[:, :, :, 128:129], 1.0).then_inc(sig("edges_ready"), 1)
            pool.wait_ge(sig("edges_ready"), 2)
            pool.wait_ge(sig("a2_landed"), 16)
            for o, i in ((0, 16), (16, 0)):
                pool.tensor_copy(krw[:, :, o:o + 16], wA[:, :, C2_KR + i:C2_KR + i + 16]).then_inc(sig("krw_ready"), 1)
            pool.wait_ge(sig("uq_landed"), 32)
            uqh = uq.rearrange("p k (h c) -> p k h c", h=A_HEADS)
            for o, i in ((0, 16), (16, 0)):
                for k in range(2):
                    pool.tensor_copy(uqw[:, k, :, o:o + 16], uqh[:, k, :, NOPE + i:NOPE + i + 16]).then_inc(sig("uqw_ready"), 1)
            pool.wait_ge(sig("kr_ready"), at("kr_ready", 1))
            pool.wait_ge(sig("uqw_ready"), 4)
            pool.tensor_copy(kTa[64:96, 1:A_HEADS, :], kTa[64:96, 0:1, :].broadcast_to([ROPE, A_HEADS - 1, SEQ]))\
                .then_inc(sig("krope_spread"), 1)

        @block.scalar
        def _(act):
            def link(ins, count=[0]):
                count[0] += 1
                ins.then_inc(sig("act_chain"), 1)
                act.wait_ge(sig("act_chain"), count[0])

            act.dma_start(prow[0:NROW, :], a["rows"]).then_inc(sig("rows_landed"), 16)
            act.dma_start(frow3, a["conv_ffn"][0].rearrange("t (r c) -> r t c", c=P)).then_inc(sig("frow_landed"), 16)
            act.dma_start(gbc[:], a["norm_mix_post"][0:1, :].broadcast_to([P, D])).then_inc(sig("gbc_landed"), 16)

            def norm(r, halves=range(TB)):
                for b in halves:
                    if r == 0:
                        act.wait_ge(sig("x_landed"), 32)
                    else:
                        act.wait_ge(sig("x_ready"), 2 * (r - 1) + b + 1)
                    link(act.activation(junk[:], x_tok[:, b, :], ACT.Square, scale=D ** -0.5,
                                        accum_out=stat[:, 4 * r + b:4 * r + b + 1]))
                    if r == 0 and b == 0:
                        act.wait_ge(sig("cleared"), 8)
                    act.activation(stat[:, 4 * r + 2 + b:4 * r + 3 + b], stat[:, 4 * r + b:4 * r + b + 1], ACT.Sqrt,
                                   bias=epsc[:]).then_inc(sig("std_ready"), 1)

            def post_norm(r):
                for b in range(TB):
                    act.wait_ge(sig("y_done"), 2 * r + b + 1)
                    c = 40 + 4 * r + b
                    link(act.activation(junk[:], ps[:, 4 + 2 * b:6 + 2 * b, :], ACT.Square, scale=D ** -0.5,
                                        accum_out=stat[:, c:c + 1]))
                    act.activation(stat[:, c + 2:c + 3], stat[:, c:c + 1], ACT.Sqrt,
                                   bias=epsc[:]).then_inc(sig("ystd_ready"), 1)

            norm(0)
            act.wait_ge(sig("lr_done"), at("lr_done", 1))
            act.copy(lr[0:RANK], ps[0:RANK, 2, :].rearrange("p (d t) -> p d t", d=2)).then_inc(sig("lr_ready"), 1)
            act.wait_ge(sig("q_done"), at("q_done", 1))
            act.mul(qT, ps[:, 3, :], 0.125).then_inc(sig("q_ready"), 1)
            act.wait_ge(sig("z_ready"), at("z_ready", 2))
            link(act.activation(t1, zz, ACT.Abs))
            link(act.activation(t1, t1, ACT.Exp, scale=-1.0))
            act.activation(t1, t1, ACT.Ln, bias=1.0).then_inc(sig("ln_ready"), 1)
            act.wait_ge(sig("k_done"), at("k_done", 1))
            act.copy(kT, ps[:, 6, :]).then_inc(sig("k_ready"), 1)
            for b in range(TB):
                act.wait_ge(sig("v_done"), at("v_done", b + 1))
                act.copy(v_tok[:, b, :], ps[:, (7, 2)[b], :]).then_inc(sig("v_ready"), 1)
            act.wait_ge(sig("cum_ready"), at("cum_ready", 1))
            act.activation(E1, cum, ACT.Exp, scale=1.0 / 16).then_inc(sig("exp_ready"), 1)
            act.activation(E2, cum, ACT.Exp, scale=-1.0 / 16).then_inc(sig("exp_ready"), 1)
            act.activation(dec, tot, ACT.Exp, scale=1.0 / 16).then_inc(sig("exp_ready"), 1)
            act.wait_ge(sig("rest_ready"), 1)
            act.activation(tmp, tmp, ACT.Exp, scale=1.0 / 16).then_inc(sig("exp_ready"), 1)
            for h in range(2):
                act.wait_ge(sig("gc_done"), at("gc_done", h + 1))
                act.copy(gcT[:, 2 * h:2 * h + 2, :], ps[:, 3 + h, :]).then_inc(sig("gc_ready"), 1)
            for h in range(2):
                act.wait_ge(sig("gb_done"), at("gb_done", h + 1))
                act.copy(gbT[:, 2 * h:2 * h + 2, :], ps[:, (7, 2)[h], :]).then_inc(sig("gb_ready"), 1)
            for h in range(2):
                act.wait_ge(sig("go_done"), at("go_done", h + 1))
                act.activation(sgo[:, 2 * h:2 * h + 2, :], ps[:, 3 + h, :], ACT.Silu).then_inc(sig("sgo_ready"), 1)
            for b in range(TB):
                act.wait_ge(sig("kot_done"), at("kot_done", b + 1))
                act.copy(kot[:, b], ps[:, b, :]).then_inc(sig("kot_ready"), 1)
            act.wait_ge(sig("o_done"), at("o_done", 2))
            act.activation(v3(junk[:], 2), ps[:, 6:8, :], ACT.Square).then_inc(sig("osq_ready"), 1)
            act.wait_ge(sig("oms_ready"), at("oms_ready", 1))
            act.activation(stat[:, 28:36], stat[:, 20:28], ACT.Sqrt, scale=1.0 / P, bias=epsc[:]).then_inc(sig("ostd_ready"), 1)
            post_norm(0)
            act.wait_ge(sig("x_ready"), 2)
            act.dma_start(gbc[:], a["norm_ffn_post"][0:1, :].broadcast_to([P, D])).then_inc(sig("gbc_landed"), 16)
            norm(1)

            for j in range(4):
                b, h = divmod(j, 2)
                act.wait_ge(sig("hT_ready"), 4 + j + 1)
                o = (slice(None), slice(4 * h, 4 * h + 4), slice(b * P, b * P + P))
                act.copy(hT_hl[0][o], hT[o]).then_inc(sig("hT_high"), 1)

            def split_up(p, q, h):
                act.wait_ge(sig(f"up_landed{q}"), h * 32 + 32)
                for c in range(4):
                    if not (isinstance(p, int) and p == 0):
                        act.wait_ge(sig("up_used"), p * 4 + c - 3)
                    act.copy(w_up_hl[0][:, c], U[q][:, :, c // 2, (c % 2) * P:(c % 2 + 1) * P]).then_inc(sig("up_high"), 1)

            def conv_mlp(p, q, h, more=True):
                if more:
                    split_up(p + 1, 1 - q, h + q)
                act.wait_ge(sig("up_used"), p * 4 + 4)
                act.wait_ge(sig("cw_ready"), p + 1)
                if not (isinstance(p, int) and p == 0):
                    act.wait_ge(sig("uact_ready"), p)
                for g, c in ((0, cgt[q]), (1, cvt[q])):
                    for i in range(2):
                        w = cwp[q][:, 6 * g + 3 * i + 1:6 * g + 3 * i + 2]
                        act.activation(c[:, i, :], ps[:, 2 * q + g, 256 * i:256 * i + 256], ACT.Copy,
                                       scale=w).then_inc(sig("centre_done"), 1)
                act.wait_ge(sig(f"down_landed{q}"), h * 16 + 16)
                for i in range(2):
                    if not (isinstance(p, int) and p == 0):
                        act.wait_ge(sig("down_used"), p * 2 + i)
                    act.copy(w_dn_hl[0][:, i], DN[q][:, i]).then_inc(sig("down_high"), 1)
                act.wait_ge(sig("tap_done"), p * 8 + 9)
                act.activation(gact[q], cgt[q], ACT.Silu).then_inc(sig("gact_ready"), 1)
                act.wait_ge(sig("uact_ready"), p + 2)
                act.copy(uact_hl[0][:, q], uact[q]).then_inc(sig("uact_high"), 1)

            act.wait_ge(sig("x_ready"), 2)
            split_up(0, 0, 0)
            conv_mlp(0, 0, 0)
            with act.Fori(0, NPAIR // 2 - 1) as i:
                conv_mlp(i * 2 + 1, 1, i)
                conv_mlp(i * 2 + 2, 0, i + 1)
            conv_mlp(NPAIR - 2, 1, NPAIR // 2 - 1)
            conv_mlp(NPAIR - 1, 0, NPAIR // 2, more=False)
            post_norm(1)

            act.wait_ge(sig("x_ready"), 4)
            act.dma_start(gbc[:], a["final_norm_g_2"].rearrange("(a n) -> a n", a=1).broadcast_to([P, D])).then_inc(sig("gbc_landed"), 16)
            norm(2)
            act.wait_ge(sig("c_done"), at("c_done", 2))
            for b in range(TB):
                for n, o in ((QL, 0), (KVL, QL)):
                    c = 48 + 2 * b + (o > 0)
                    link(act.activation(junk[:, 0:n], ps[:, 2 + b, o:o + n], ACT.Square, scale=float(n) ** -0.5,
                                        accum_out=stat[:, c:c + 1]))
            act.activation(stat[:, 48:52], stat[:, 48:52], ACT.Sqrt, bias=epsc[:]).then_inc(sig("cstd_ready"), 1)
            act.wait_ge(sig("gz_ready"), at("gz_ready", 2))
            link(act.activation(gat[0:4, 2, :], gat[0:4, 1, :], ACT.Abs))
            link(act.activation(gat[0:4, 2, :], gat[0:4, 2, :], ACT.Exp, scale=-1.0))
            act.activation(gat[0:4, 2, :], gat[0:4, 2, :], ACT.Ln, bias=1.0).then_inc(sig("gln_ready"), 1)
            act.wait_ge(sig("ang_ready"), 1)
            act.activation(cosT[64:96, :], cosT[64:96, :], ACT.Sin).then_inc(sig("cs_ready"), 1)
            act.activation(sinT[64:96, :], sinT[64:96, :], ACT.Sin, scale=sgn[64:96, :]).then_inc(sig("cs_ready"), 1)
            for h in range(2):
                act.wait_ge(sig("xm_done"), at("xm_done", h + 1))
                act.copy(xmT[:, 2 * h:2 * h + 2, 3:259], v3(ps[:, 6 + h, :], 2)).then_inc(sig("xm_ready"), 1)
            for h in range(2):
                act.wait_ge(sig("z2_done"), at("z2_done", h + 1))
                act.activation(szT[:, 2 * h:2 * h + 2, :], v3(ps[:, 2 + h, :], 2), ACT.Silu).then_inc(sig("sz_ready"), 1)
            for h in range(M_HEADS):
                act.wait_ge(sig("conv2_done"), at("conv2_done", h + 1))
                act.activation(xcT[:, h, :], xcT[:, h, :], ACT.Silu, bias=par_c("conv_b_2", h)).then_inc(sig("xc_ready"), 1)
            for hp in range(4):
                act.wait_ge(sig("qa_done"), at("qa_done", hp + 1))
                act.copy(qTa[0:64, 2 * hp:2 * hp + 2, :], v3(ps[0:64, 2 * (hp % 2), :], 2)).then_inc(sig("qn_ready"), 1)
            for hp in range(4):
                act.wait_ge(sig("ka_done"), at("ka_done", hp + 1))
                act.copy(kTa[0:64, 2 * hp:2 * hp + 2, :], v3(ps[0:64, 4 + hp, :], 2)).then_inc(sig("kn_ready"), 1)
            for b in range(TB):
                act.wait_ge(sig("v2_done"), at("v2_done", b + 1))
                act.copy(v2[:, b, :], ps[:, b, :]).then_inc(sig("v2_ready"), 1)
            act.wait_ge(sig("ucol_ready"), at("ucol_ready", 1))
            act.activation(ufl, ufl, ACT.Exp, scale=-1.0).then_inc(sig("floor_ready"), 1)
            for h in range(2):
                act.wait_ge(sig("mq_done"), at("mq_done", h + 1))
                act.copy(mqT[:, 2 * h:2 * h + 2, :], v3(ps[:, 6 + h, :], 2)).then_inc(sig("mq_ready"), 1)
            for h in range(2):
                act.wait_ge(sig("mk_done"), at("mk_done", h + 1))
                act.mul(mkT[:, 2 * h:2 * h + 2, :], v3(ps[:, h, :], 2), float(P) ** -0.5).then_inc(sig("mk_ready"), 1)
            for b in range(TB):
                act.wait_ge(sig("mv_done"), at("mv_done", b + 1))
                act.copy(vext[:, b, :, 0:128], v3(ps[:, 3 - b, :], 4)).then_inc(sig("mv_ready"), 1)
            for h in range(M_HEADS):
                act.wait_ge(sig("warg_ready"), h + 1)
                act.activation(wexp[:, h, :], wexp[:, h, :], ACT.Exp).then_inc(sig("wexp_ready"), 1)
            for i in range(2 * 4 + 2):
                if i < 8:
                    b = i % 2
                    nk = P * (b + 1)
                    act.wait_ge(sig("s_ready"), i + 1)
                    for hh in range(2):
                        act.activation(sP[i % 2][:, hh, 0:nk], sP[i % 2][:, hh, 0:nk], ACT.Exp,
                                       bias=amx[i % 2][:, hh:hh + 1], accum_out=asum[i % 2][:, hh:hh + 1])\
                           .then_inc(sig("e_ready"), 1)
                if 1 <= i <= 8:
                    act.wait_ge(sig("pt_done"), i)
                    if i >= 3:
                        act.wait_ge(sig("pv_done"), i - 2)
                    n = 2 * ((i - 1) % 2 + 1)
                    act.copy(PTs[(i - 1) % 2][:, 0:n, :], v3(ps[:, 2 + (i - 1) % 2, 0:n * P], n)).then_inc(sig("PTs_ready"), 1)
                if i >= 2 and i % 2 == 1:
                    hp = (i - 2) // 2
                    act.wait_ge(sig("pv_done"), i - 1)
                    act.copy(hT[:, hp, :], ps[:, 4 + hp % 2, 0:256]).then_inc(sig("at_ready"), 1)
            for h in range(M_HEADS):
                act.activation(xcT[:, h, :], xcT[:, h, :], ACT.Copy, scale=par_c("ml_skip_2", h)).then_inc(sig("skip_ready"), 1)
            act.wait_ge(sig("mvar_ready"), 1)
            act.activation(mstd, mstd, ACT.Sqrt, bias=epsc[:]).then_inc(sig("mstd_ready"), 1)
            norm(3)
            act.wait_ge(sig("gsub_ready"), at("gsub_ready", 1))
            act.activation(g4[1], g4[1], ACT.Exp).then_inc(sig("rt_exp"), 1)
            act.wait_ge(sig("msub_ready"), at("msub_ready", 1))
            act.activation(sm[4], sm[4], ACT.Exp).then_inc(sig("rt_exp"), 1)

            act.wait_ge(sig("rounds_ready"), 1)
            rounds = act.value_load(nri[0:1, :], min_val=1, max_val=SEQ // CAP)
            for name in ("sc_ready", "sg_ready", "ypa_ready", "aT_ready"):
                act.sem_inc(sig(name), 2)

            def scatter_out(n, q):
                act.wait_ge(sig("oht_done"), n + 3)
                act.copy(SC[q], ps[:, 3, 0:256]).then_inc(sig("sc_ready"), 1)

            def expert_act(n, q):
                act.wait_ge(sig("u_done"), n + 3)
                act.activation(sg[q], ps[:, 2, 0:F_EXP], ACT.Silu).then_inc(sig("sg_ready"), 1)

            def rows_out(n, q):
                act.wait_ge(sig("d_done"), n + 3)
                act.copy(Yp[q][:, 0, :], ps[:, 3, :]).then_inc(sig("ypa_ready"), 1)

            def act_step(n, q, more=True):
                expert_act(n, q)
                act.wait_ge(sig("at_done"), n + 3)
                if more:
                    scatter_out(n + 1, 1 - q)
                act.copy(aT[q], v3(ps[:, 3, 256:512], 2)).then_inc(sig("aT_ready"), 1)
                rows_out(n, q)

            with act.Fori(0, rounds) as r:
                scatter_out(r * NEP, 0)
                act_step(r * NEP, 0)
                with act.Fori(0, NEP // 2 - 1) as i:
                    act_step(r * NEP + i * 2 + 1, 1)
                    act_step(r * NEP + i * 2 + 2, 0)
                act_step(r * NEP + NEP - 1, 1, more=False)

            norm(4)
            for b in range(TB):
                for half in range(2):
                    act.wait_ge(sig("pg_done"), 2 * b + half + 1)
                    act.activation(sgate[:, b, 512 * half:512 * half + 512], ps[:, 4 + 2 * b + half, :],
                                   ACT.Sigmoid).then_inc(sig("sgate_ready"), 1)
                norm(5, (b,))

        @block.vector
        def _(dve):
            def link(ins, count=[0]):
                count[0] += 1
                ins.then_inc(sig("dve_chain"), 1)
                dve.wait_ge(sig("dve_chain"), count[0])

            dve.wait_ge(sig("par_done"), 1)
            link(dve.tensor_copy(par[:, 0:NROW], ps[:, 7, 0:NROW]))
            for t in range(3):
                dve.tensor_copy(cw.rearrange("p (r g i t) -> p t g r i", g=2, i=2, t=3)[:, t],
                                ps[:, 7, 128 + 44 * t:172 + 44 * t].rearrange("p (g r i) -> p g r i", g=2, i=2)) \
                   .then_inc(sig("params_out"), 1)

            def norm(r, gain):
                for b in range(TB):
                    std = stat[:, 4 * r + 2 + b:4 * r + 3 + b]
                    dve.wait_ge(sig("std_ready"), 2 * r + b + 1)
                    link(dve.reciprocal(std, std))
                    dve.tensor_scalar(hn[:, b, :], x_tok[:, b, :], stat[:, 4 * r + 2 + b:4 * r + 3 + b], None,
                                      ALU.mult).then_inc(sig("hn_ready"), 1)
                for j in range(4):
                    b, h = divmod(j, 2)
                    dve.wait_ge(sig("hT_done"), 4 * r + j + 1)
                    dve.tensor_tensor(hT[:, 4 * h:4 * h + 4, b * P:(b + 1) * P],
                                      ps[:, h, :].rearrange("p (k t) -> p k t", k=4),
                                      par_c(gain, 4 * h, 4).unsqueeze(2).broadcast_to([P, 4, P]),
                                      ALU.mult).then_inc(sig("hT_ready"), 1)

            def post_norm(r):
                dve.wait_ge(sig("gbc_landed"), 16 * (r + 1))
                for b in range(TB):
                    c = 42 + 4 * r + b
                    dve.wait_ge(sig("ystd_ready"), 2 * r + b + 1)
                    link(dve.reciprocal(stat[:, c:c + 1], stat[:, c:c + 1]))
                    link(dve.scalar_tensor_tensor(hn[:, b, :], ps[:, 4 + 2 * b:6 + 2 * b, :].rearrange("p a b -> p (a b)"),
                                                  stat[:, c:c + 1], gbc[:], ALU.mult, ALU.mult))
                    dve.tensor_tensor(x_tok[:, b, :], x_tok[:, b, :], hn[:, b, :], ALU.add).then_inc(sig("x_ready"), 1)

            norm(0, "norm_mix_pre")
            for d, name in enumerate(("gate_bias_fwd", "gate_bias_bwd")):
                dve.wait_ge(sig("pre_done"), at("pre_done", d + 1))
                dve.tensor_tensor(v3(zz[:, d, :], 2), v3(ps[:, 4 + d, :], 2),
                                  par_c(name, 0, 2).unsqueeze(2).broadcast_to([P, 2, SEQ]), ALU.add).then_inc(sig("z_ready"), 1)
            dve.wait_ge(sig("z_ready"), at("z_ready", 2))
            dve.wait_ge(sig("ln_ready"), at("ln_ready", 1))
            link(dve.scalar_tensor_tensor(la, zz, 0.0, t1, ALU.min, ALU.subtract))
            dve.wait_ge(sig("rmask_ready"), 1)
            link(dve.tensor_tensor_scan(cum[:, 0, :], rmask, la[:, 0, :], 0.0, ALU.mult, ALU.add))
            link(dve.tensor_tensor_scan(cum[:, 1, :], rmask, la[:, 1, :], 0.0, ALU.mult, ALU.add))
            cum4 = cum.rearrange("p d (c t) -> p (d c) t", t=CH)
            link(dve.tensor_copy(tot, cum.rearrange("p d (c t) -> p d c t", t=CH)[:, :, :, CH - 1]))
            totf = tot.rearrange("p d c -> p (d c)")
            dve.tensor_tensor(v3(tmp[:, 0, :], 8), totf[:, 0:8].unsqueeze(2).broadcast_to([P, 8, CH]),
                              v3(cum[:, 0, :], 8), ALU.subtract).then_inc(sig("rest_half"), 1)
            link(dve.tensor_tensor(tmp[:, 1, :], cum[:, 1, :], la[:, 1, :], ALU.subtract))
            dve.tensor_tensor(v3(cum[:, 1, :], 8), totf[:, 8:16].unsqueeze(2).broadcast_to([P, 8, CH]),
                              v3(tmp[:, 1, :], 8), ALU.subtract).then_inc(sig("cum_ready"), 1)
            dve.wait_ge(sig("rest_half"), at("rest_half", 1))
            dve.sem_inc(sig("rest_ready"), 1)
            dve.wait_ge(sig("q_ready"), at("q_ready", 1))
            dve.wait_ge(sig("k_ready"), at("k_ready", 1))
            for s, (dst, src, e) in enumerate(((q_in, qT, E1), (k_in, kT, E2), (k_out, kT, tmp))):
                dve.wait_ge(sig("exp_ready"), at("exp_ready", (1, 2, 4)[s]))
                for d in range(2):
                    dve.tensor_tensor(dst[:, d, :], src, e[:, d, :], ALU.mult).then_inc(sig("qk_ready"), 1)
            for h in range(2):
                dve.wait_ge(sig("gc_ready"), at("gc_ready", h + 1))
                dve.wait_ge(sig("gv_done"), at("gv_done", h + 1))
                dve.tensor_tensor(mT[:, 2 * h:2 * h + 2, 1:257], v3(ps[:, 5 + h, :], 2), gcT[:, 2 * h:2 * h + 2, :],
                                  ALU.mult).then_inc(sig("m_ready"), 1)
            dve.wait_ge(sig("m_ready"), at("m_ready", 2))
            for tap in range(3):
                for t in range(4):
                    w = par_c("conv_a", 4 * tap + t)
                    src = mT[:, t, tap:tap + 256]
                    if tap == 0:
                        ins = dve.tensor_scalar(cv[:, t, :], src, w, None, ALU.mult)
                    else:
                        ins = dve.scalar_tensor_tensor(cv[:, t, :], src, w, cv[:, t, :], ALU.mult, ALU.add)
                    if t == 3:
                        link(ins)
                    else:
                        ins.then_inc(sig("conv_a"), 1)
                dve.wait_ge(sig("conv_a"), at("conv_a", 3 * (tap + 1)))
            dve.wait_ge(sig("gb_ready"), at("gb_ready", 2))
            dve.wait_ge(sig("go_done"), at("go_done", 2))
            dve.tensor_tensor(yT[:, 0:4, :], cv, gbT, ALU.mult).then_inc(sig("ya_ready"), 1)
            dve.wait_ge(sig("mask_cut"), 4)
            for g in range(4):
                b, hh = divmod(g, 2)
                dve.wait_ge(sig("scores_done"), at("scores_done", g + 1))
                link(dve.tensor_tensor(tmpP, v4(ps[:, (5, 6, 7, 2)[g], :], 2, 2),
                                       mask2[:].unsqueeze(1).broadcast_to([P, 2, 2, P]), ALU.mult))
                dve.tensor_tensor(PT[:, b, hh:4:2, :], tmpP[:, :, 0, :], tmpP[:, :, 1, :],
                                  ALU.add).then_inc(sig("PT_ready"), 1)
                dve.wait_ge(sig("PT_ready"), at("PT_ready", g + 1))
            dec4 = dec.rearrange("p d (j c) -> p d j c", j=2)
            for k in range(3):
                dve.wait_ge(sig("kv_done"), at("kv_done", 3))
                for d in range(2):
                    bank, o = KV_AT[d][k]
                    kv = v3(ps[:, bank, o:o + 256], 2)
                    if k == 0:
                        ins = dve.tensor_copy(S_st[:, 3 * d], kv)
                        link(ins)
                        continue
                    c = (k, 3 - k)[d]
                    for j in range(2):
                        link(dve.scalar_tensor_tensor(S_st[:, 3 * d + k, j, :], S_st[:, 3 * d + k - 1, j, :],
                                                      dec4[:, d, j, c:c + 1], kv[:, j, :], ALU.mult, ALU.add))
                dve.sem_inc(sig("S_ready"), 1)
            dve.wait_ge(sig("osq_ready"), at("osq_ready", 1))
            dve.tensor_reduce(stat[:, 20:28], v3(junk[:], 8), AX, ALU.add).then_inc(sig("oms_ready"), 1)
            dve.wait_ge(sig("ostd_ready"), at("ostd_ready", 1))
            link(dve.reciprocal(stat[:, 28:36], stat[:, 28:36]))
            for b in range(TB):
                dve.tensor_tensor(on[:, b, :].rearrange("p (j h c) -> p h j c", j=2, h=2), o_ps(b),
                                  v4(stat[:, 28:36], 2, 2)[:, :, b, :].unsqueeze(3).broadcast_to([P, 2, 2, P]),
                                  ALU.mult).then_inc(sig("on_ready"), 1)
            dve.wait_ge(sig("sgo_ready"), at("sgo_ready", 2))
            for b in range(TB):
                dve.wait_ge(sig("onT_done"), at("onT_done", b + 1))
                dve.scalar_tensor_tensor(yT[:, 4:8, b * P:(b + 1) * P], v3(ps[:, b, :], 4), par_c("gla_head_norm", 0),
                                         sgo[:, :, b * P:(b + 1) * P], ALU.mult, ALU.mult).then_inc(sig("yb_ready"), 1)
            post_norm(0)
            norm(1, "norm_ffn_pre")

            for j in range(4):
                b, h = divmod(j, 2)
                o = (slice(None), slice(4 * h, 4 * h + 4), slice(b * P, b * P + P))
                dve.wait_ge(sig("hT_high"), j + 1)
                dve.tensor_tensor(hT_hl[1][o], hT[o], hT_hl[0][o].bitcast(F32), ALU.subtract).then_inc(sig("hT_low"), 1)

            def split_up(p, q):
                for c in range(4):
                    dve.wait_ge(sig("up_high"), p * 4 + c + 1)
                    dve.tensor_tensor(w_up_hl[1][:, c], U[q][:, :, c // 2, (c % 2) * P:(c % 2 + 1) * P],
                                      w_up_hl[0][:, c].bitcast(F32), ALU.subtract).then_inc(sig("up_low"), 1)

            def conv_mlp(p, q, h, more=True):
                if more:
                    split_up(p + 1, 1 - q)
                if not (isinstance(p, int) and p == 0):
                    dve.wait_ge(sig("tap_done"), p * 8 + 1)
                dve.tensor_copy(cwp[q], cw[:, bass.ds(p * 12, 12)]).then_inc(sig("cw_ready"), 1)
                dve.wait_ge(sig("centre_done"), p * 4 + 4)
                dve.wait_ge(sig("cw_ready"), p + 1)
                for side in range(2):
                    for g, c in ((0, cgt[q]), (1, cvt[q])):
                        for i in range(2):
                            w = cwp[q][:, 6 * g + 3 * i + 2 * side:6 * g + 3 * i + 2 * side + 1]
                            u = ps[:, 2 * q + g, 256 * i:256 * i + 256]
                            if side == 0:
                                o, s = c[:, i, 1:256], u[:, 0:255]
                            else:
                                o, s = c[:, i, 0:255], u[:, 1:256]
                            dve.scalar_tensor_tensor(o, s, w, o, ALU.mult, ALU.add).then_inc(sig("tap_done"), 1)
                    dve.wait_ge(sig("tap_done"), p * 8 + 5 + 4 * side)
                for i in range(2):
                    dve.wait_ge(sig("down_high"), p * 2 + i + 1)
                    dve.tensor_tensor(w_dn_hl[1][:, i], DN[q][:, i], w_dn_hl[0][:, i].bitcast(F32),
                                      ALU.subtract).then_inc(sig("down_low"), 1)
                dve.wait_ge(sig("gact_ready"), p + 1)
                dve.tensor_tensor(uact[q], gact[q], cvt[q], ALU.mult).then_inc(sig("uact_ready"), 1)
                dve.wait_ge(sig("uact_ready"), p + 2)
                dve.wait_ge(sig("uact_high"), p + 1)
                dve.tensor_tensor(uact_hl[1][:, q], uact[q], uact_hl[0][:, q].bitcast(F32), ALU.subtract)\
                   .then_inc(sig("uact_low"), 1)

            dve.wait_ge(sig("params_out"), 3)
            dve.sem_inc(sig("tap_done"), 1)
            dve.sem_inc(sig("uact_ready"), 1)
            split_up(0, 0)
            conv_mlp(0, 0, 0)
            with dve.Fori(0, NPAIR // 2 - 1) as i:
                conv_mlp(i * 2 + 1, 1, i)
                conv_mlp(i * 2 + 2, 0, i + 1)
            conv_mlp(NPAIR - 2, 1, NPAIR // 2 - 1)
            conv_mlp(NPAIR - 1, 0, NPAIR // 2, more=False)
            post_norm(1)

            norm(2, "norm_mix_g_2")
            R0, R1 = 64, 96
            dve.wait_ge(sig("small_landed"), 16 * 9)
            dve.wait_ge(sig("icol_done"), at("icol_done", 1))
            dve.tensor_copy(icol[R0:R1], ps[R0:R1, 7, 0:1]).then_inc(sig("icol_ready"), 1)
            dve.wait_ge(sig("icol_ready"), at("icol_ready", 1))
            link(dve.tensor_copy(ang[R0:R1, :], posi[R0:R1, :].bitcast(I32)))
            link(dve.tensor_scalar(ang[R0:R1, :], ang[R0:R1, :], icol[R0:R1], None, ALU.mult))
            TWO_PI = 2 * np.pi
            HI = 6.28125
            LO = float(TWO_PI - HI)
            MAGIC = 12582912.0
            LIM = 3.1415925
            for dst, turn in ((sinT, 0.0), (cosT, 0.25)):
                t = dst[R0:R1, :]
                link(dve.tensor_scalar(t, ang[R0:R1, :], float(1 / TWO_PI), turn, ALU.mult, ALU.add))
                link(dve.tensor_scalar(t, t, MAGIC, MAGIC, ALU.add, ALU.subtract))
                link(dve.scalar_tensor_tensor(angr[R0:R1, :], t, -HI, ang[R0:R1, :], ALU.mult, ALU.add))
                link(dve.scalar_tensor_tensor(t, t, -LO, angr[R0:R1, :], ALU.mult, ALU.add))
                if turn:
                    link(dve.tensor_scalar(t, t, float(np.pi / 2), None, ALU.add))
                link(dve.tensor_scalar(t, t, LIM, -LIM, ALU.min, ALU.max))
            dve.sem_inc(sig("ang_ready"), 1)
            dve.wait_ge(sig("cstd_ready"), at("cstd_ready", 1))
            link(dve.reciprocal(stat[:, 48:52], stat[:, 48:52]))
            for b in range(TB):
                for n, o in ((QL, 0), (KVL, QL)):
                    c = 48 + 2 * b + (o > 0)
                    dve.tensor_scalar(cn[:, b, o:o + n], ps[:, 2 + b, o:o + n], stat[:, c:c + 1], None,
                                      ALU.mult).then_inc(sig("cn_ready"), 1)
            gi, gz, gl, gb = (gat[0:4, n, :] for n in range(4))
            dve.wait_ge(sig("if_done"), at("if_done", 1))
            for n in range(2):
                dve.tensor_scalar(gat[0:4, n, :], ps[0:4, 5, 256 * n:256 * n + 256], bif[0:4, n:n + 1], None,
                                  ALU.add).then_inc(sig("gz_ready"), 1)
            for b in range(TB):
                dve.wait_ge(sig("cT_done"), at("cT_done", b + 1))
                dve.tensor_tensor(cT[:, :, b * P:(b + 1) * P], v3(ps[:, b, 0:384], 3),
                                  par_c("q_norm_g_2", 0, 3).unsqueeze(2).broadcast_to([P, 3, P]), ALU.mult)\
                   .then_inc(sig("cT_ready"), 1)
            dve.wait_ge(sig("gz_ready"), at("gz_ready", 2))
            dve.wait_ge(sig("gln_ready"), at("gln_ready", 1))
            link(dve.scalar_tensor_tensor(gz, gz, 0.0, gl, ALU.min, ALU.subtract))
            link(dve.tensor_tensor_scan(gb, onesr[0:4], gz, 0.0, ALU.mult, ALU.add))
            link(dve.tensor_tensor(gi, gi, gb, ALU.subtract))
            link(dve.tensor_tensor_scan(gz, onesr[0:4], gi, 0.0, ALU.mult, ALU.max))
            dve.tensor_tensor(gb, gb, gz, ALU.add).then_inc(sig("gates_ready"), 1)
            for h in range(M_HEADS):
                dve.wait_ge(sig("xm_ready"), at("xm_ready", h // 2 + 1))
                for tap in range(4):
                    w = par_c("conv_w_2", 4 * tap + h)
                    src = xmT[:, h, tap:tap + 256]
                    if tap == 0:
                        link(dve.tensor_scalar(xcT[:, h, :], src, w, None, ALU.mult))
                    elif tap < 3:
                        link(dve.scalar_tensor_tensor(xcT[:, h, :], src, w, xcT[:, h, :], ALU.mult, ALU.add))
                    else:
                        dve.scalar_tensor_tensor(xcT[:, h, :], src, w, xcT[:, h, :], ALU.mult, ALU.add)\
                           .then_inc(sig("conv2_done"), 1)

            def rope(dst, plain, swapped, n, signal):
                c, s_ = (v[R0:R1, :].unsqueeze(1).broadcast_to([ROPE, n, SEQ]) for v in (cosT, sinT))
                link(dve.tensor_tensor(rt[0], plain, c, ALU.mult))
                link(dve.tensor_tensor(rt[1], swapped, s_, ALU.mult))
                dve.tensor_tensor(dst, rt[0], rt[1], ALU.add).then_inc(sig(signal), 1)
                dve.wait_ge(sig(signal), at(signal, rope_n.setdefault(signal, 0) + 1))
                rope_n[signal] += 1

            rope_n = {}
            dve.wait_ge(sig("cs_ready"), at("cs_ready", 2))
            dve.wait_ge(sig("kr_done"), at("kr_done", 1))
            rt = [v3(t[R0:R1, 0:256], 1) for t in rtb]
            rope(kTa[R0:R1, 0:1, :], v3(ps[R0:R1, 4, 0:256], 1), v3(ps[R0:R1, 4, 256:512], 1), 1, "kr_ready")
            rt = [v3(t[R0:R1, :], 2) for t in rtb]
            for hp in range(4):
                dve.wait_ge(sig("qa_done"), at("qa_done", hp + 1))
                bank = 2 * (hp % 2)
                rope(qTa[R0:R1, 2 * hp:2 * hp + 2, :], v3(ps[R0:R1, bank, :], 2), v3(ps[R0:R1, bank + 1, :], 2), 2, "qr_ready")
            dve.wait_ge(sig("gT_done"), at("gT_done", 1))
            link(dve.tensor_copy(ucol, ps[:, 2, 0:8]))
            dve.tensor_copy(ufl, ps[:, 2, 8:16]).then_inc(sig("ucol_ready"), 1)
            for h in range(M_HEADS):
                dve.wait_ge(sig("negM_done"), at("negM_done", h // 2 + 1))
                m = ps[:, 4 + h // 2, 256 * (h % 2):256 * (h % 2) + 256]
                dve.scalar_tensor_tensor(wexp[:, h, 0:256], m, ucol[:, h:h + 1], cmask, ALU.add, ALU.add)\
                   .then_inc(sig("warg_half"), 1)
                dve.scalar_tensor_tensor(wexp[:, h, 256:384], m[:, 128:256], ucol[:, 4 + h:5 + h], cmask[:, 0:P],
                                         ALU.add, ALU.add).then_inc(sig("warg_ready"), 1)
            dve.wait_ge(sig("warg_half"), 4)
            dve.sem_inc(sig("warg_all"), 1)

            def softmax_in(i):
                b = i % 2
                nk = P * (b + 1)
                dve.wait_ge(sig("s_done"), i + 1)
                if i >= 2:
                    dve.wait_ge(sig("pt_done"), i - 1)
                m = amask[:, P:2 * P] if b == 0 else amask
                link(dve.scalar_tensor_tensor(sP[i % 2][:, :, 0:nk], v3(ps[:, i % 2, 0:2 * nk], 2), A_SCALE,
                                              m.unsqueeze(1).broadcast_to([P, 2, nk]), ALU.mult, ALU.add))
                dve.tensor_reduce(amx[i % 2], sP[i % 2][:, :, 0:nk], AX, ALU.max, negate=True).then_inc(sig("s_ready"), 1)

            def softmax_out(i):
                nk = P * (i % 2 + 1)
                dve.wait_ge(sig("e_ready"), 2 * i + 2)
                link(dve.reciprocal(asum[i % 2], asum[i % 2]))
                dve.tensor_tensor(sP[i % 2][:, :, 0:nk], sP[i % 2][:, :, 0:nk],
                                  asum[i % 2].unsqueeze(2).broadcast_to([P, 2, nk]), ALU.mult).then_inc(sig("p_ready"), 1)

            for i in range(9):
                if i < 8:
                    softmax_in(i)
                if i >= 1:
                    softmax_out(i - 1)
                h = i // 2
                if i < 8 and i % 2 == 0:
                    dve.wait_ge(sig("qk_done"), h + 1)
                    dve.wait_ge(sig("wexp_ready"), at("wexp_ready", h + 1))
                    dve.tensor_tensor(pm[h % 2], ps[:, 6, 0:384], wexp[:, h, :], ALU.mult).then_inc(sig("pm_ready"), 1)
                if i < 8 and i % 2 == 1:
                    dve.wait_ge(sig("num_done"), h + 1)
                    if h == 0:
                        dve.wait_ge(sig("floor_ready"), at("floor_ready", 1))
                    nd = ps[:, 7, 0:258].rearrange("p (b e) -> p b e", b=2)
                    den = hden[:, 0:2]
                    link(dve.tensor_copy(den.unsqueeze(2), nd[:, :, 128:129]))
                    link(dve.scalar_tensor_tensor(den, den, -1.0, den, ALU.mult, ALU.max))
                    link(dve.tensor_tensor(den.unsqueeze(2), den.unsqueeze(2),
                                           ufl.rearrange("p (b h) -> p b h", b=2)[:, :, h:h + 1], ALU.max))
                    link(dve.reciprocal(den, den))
                    dve.tensor_tensor(hmt.rearrange("p b (h e) -> p b h e", h=4)[:, :, h, :], nd[:, :, 0:128],
                                      den.unsqueeze(2).broadcast_to([P, 2, P]), ALU.mult).then_inc(sig("hm_ready"), 1)
                    dve.wait_ge(sig("hm_ready"), h + 1)
                    for b in range(TB):
                        link(dve.bn_stats(bns[:, 2 * h + b, :], hmt[:, b, h * P:(h + 1) * P]))
                        link(dve.bn_aggr(mmv[:, 2 * h + b, :], bns[:, 2 * h + b, :]))
            link(dve.tensor_copy(mstd, mmv[:, :, 1]))
            dve.sem_inc(sig("mvar_ready"), 1)
            dve.wait_ge(sig("mstd_ready"), 1)
            link(dve.reciprocal(mstd, mstd))
            for b in range(TB):
                for h in range(M_HEADS):
                    v = hmt[:, b, h * P:(h + 1) * P]
                    dve.tensor_scalar(v, v, mmv[:, 2 * h + b, 0:1], mstd[:, 2 * h + b:2 * h + b + 1],
                                      ALU.subtract, ALU.mult).then_inc(sig("hmn_ready"), 1)
            dve.wait_ge(sig("skip_ready"), 4)
            for b in range(TB):
                dve.wait_ge(sig("hmT_done"), at("hmT_done", b + 1))
                y = hT[:, 4:8, b * P:(b + 1) * P]
                link(dve.tensor_tensor(y, v3(ps[:, 6 + b, :], 4),
                                       par_c("mh_norm_g_2", 0, 4).unsqueeze(2).broadcast_to([P, 4, P]), ALU.mult))
                link(dve.tensor_tensor(y, y, xcT[:, :, b * P:(b + 1) * P], ALU.add))
                dve.tensor_tensor(y, y, szT[:, :, b * P:(b + 1) * P], ALU.mult).then_inc(sig("ym_ready"), 1)
            for b in range(TB):
                dve.wait_ge(sig("y2_done"), at("y2_done", b + 1))
                dve.tensor_tensor(x_tok[:, b, :], x_tok[:, b, :],
                                  ps[:, 4 + 2 * b:6 + 2 * b, :].rearrange("p a b -> p (a b)"), ALU.add).then_inc(sig("x_ready"), 1)
            norm(3, "norm_ffn_g_2")

            dve.memset(RK, -1.0).then_inc(sig("rt_clear"), 1)
            dve.memset(WK, 0.0).then_inc(sig("rt_clear"), 1)
            dve.wait_ge(sig("rt_clear"), at("rt_clear", 2))
            dve.wait_ge(sig("logits_done"), at("logits_done", 1))
            link(dve.tensor_tensor(Lg, ps[:, 2, 0:72].rearrange("p (b n) -> p b n", b=2),
                                   brt.unsqueeze(1).broadcast_to([P, 2, 36]), ALU.add))
            gl_, el_ = Lg[:, :, 0:N_GRP], Lg[:, :, N_GRP:36]
            io4 = iot[:, 0:N_GRP].unsqueeze(1).broadcast_to([P, 2, N_GRP])
            io32 = iot[:, 0:N_EXP].unsqueeze(1).broadcast_to([P, 2, N_EXP])

            def wide(t, n):
                return t.unsqueeze(2).broadcast_to([P, 2, n])

            def first_max(vals, top, hot, io, n):
                link(dve.tensor_reduce(top, vals, AX, ALU.max))
                link(dve.tensor_tensor(hot, vals, wide(top, n), ALU.is_equal))
                link(dve.scalar_tensor_tensor(hot, hot, -64.0, io, ALU.mult, ALU.add))
                link(dve.tensor_reduce(sm[11], hot, AX, ALU.min))
                link(dve.tensor_tensor(hot, hot, wide(sm[11], n), ALU.is_equal))

            dve.wait_ge(sig("pT_done"), at("pT_done", 1))
            dve.tensor_copy(pT, v3(ps[:, 0, :], 2)).then_inc(sig("pT_ready"), 1)

            first_max(gl_, sm[0], g4[0], io4, N_GRP)
            dve.tensor_tensor(g4[1], gl_, wide(sm[0], N_GRP), ALU.subtract).then_inc(sig("gsub_ready"), 1)
            link(dve.tensor_scalar(g4[2], g4[0], -NEG, NEG, ALU.mult, ALU.add))
            em = e32[0]
            link(dve.tensor_tensor(em.rearrange("p b (g e) -> p b g e", g=N_GRP),
                                   el_.rearrange("p b (g e) -> p b g e", g=N_GRP),
                                   g4[2].unsqueeze(3).broadcast_to([P, 2, N_GRP, EPG]), ALU.add))
            first_max(em, sm[1], e32[1], io32, N_EXP)
            link(dve.scalar_tensor_tensor(em, e32[1], 3 * NEG, em, ALU.mult, ALU.add))
            first_max(em, sm[2], e32[2], io32, N_EXP)
            dve.tensor_tensor(sm[4], sm[2], sm[1], ALU.subtract).then_inc(sig("msub_ready"), 1)
            dve.wait_ge(sig("rt_exp"), 2)
            link(dve.tensor_reduce(sm[5], g4[1], AX, ALU.add))
            link(dve.scalar_tensor_tensor(sm[5], sm[4], 1.0, sm[5], ALU.add, ALU.mult))
            link(dve.reciprocal(sm[6], sm[5]))
            link(dve.tensor_tensor(sm[7], sm[6], sm[4], ALU.mult))
            dve.tensor_tensor(e32[3], e32[1], e32[2], ALU.add).then_inc(sig("sel_ready"), 1)
            link(dve.tensor_tensor(e32[1], e32[1], wide(sm[6], N_EXP), ALU.mult))
            link(dve.tensor_tensor(e32[2], e32[2], wide(sm[7], N_EXP), ALU.mult))
            link(dve.tensor_tensor(WK.rearrange("p (e b) -> p b e", b=2), e32[1], e32[2], ALU.add))
            dve.wait_ge(sig("rank_done"), at("rank_done", 1))
            dve.wait_ge(sig("sel_ready"), at("sel_ready", 1))
            link(dve.scalar_tensor_tensor(e32[4], v3(ps[:, 3, 0:64], 2), 1.0, e32[3], ALU.add, ALU.mult))
            link(dve.tensor_scalar(RK.rearrange("p (e b) -> p b e", b=2), e32[4], -1.0, None, ALU.add))
            link(dve.tensor_reduce(nrf[:, 0:1], ps[:, 3, 64:96], AX, ALU.max))
            for n in range(SEQ // CAP):
                link(dve.tensor_scalar(nrf[:, 1 + (n > 0):2 + (n > 0)], nrf[:, 0:1], CAP * n + 0.5, None, ALU.is_gt))
                if n:
                    link(dve.tensor_tensor(nrf[:, 1:2], nrf[:, 1:2], nrf[:, 2:3], ALU.add))
            dve.tensor_copy(nri, nrf[:, 1:2]).then_inc(sig("rounds_ready"), 1)
            dve.wait_ge(sig("rounds_ready"), 1)
            rounds = dve.value_load(nri[0:1, :], min_val=1, max_val=SEQ // CAP)

            for name in ("oh_ready", "xg_ready", "a_ready", "ypb_ready"):
                dve.sem_inc(sig(name), 2)
            dve.sem_inc(sig("cols_ready"), 2)

            def one_hot(n, t, q):
                dve.wait_ge(sig("g_done"), n + 1)
                dve.tensor_copy(rkp[q], RK[:, bass.ds(t * 4, 4)]).then_inc(sig("rk_ready"), 1)
                dve.tensor_copy(wkp[q], WK[:, bass.ds(t * 4, 4)]).then_inc(sig("cols_ready"), 1)
                dve.wait_ge(sig("rk_ready"), n + 1)
                dve.wait_ge(sig("cols_ready"), n + 3)
                for e in range(2):
                    for b in range(TB):
                        r_, w_ = (v[q][:, 2 * e + b:2 * e + b + 1] for v in (rkp, wkp))
                        o = slice(CAP * e, CAP * e + CAP)
                        dve.tensor_scalar(OH[q][:, b, o], iot, r_, None, ALU.is_equal).then_inc(sig("oh_part"), 1)
                        ins = dve.tensor_scalar(OHW[q][:, b, o], iot, r_, w_, ALU.is_equal, ALU.mult)
                        ins.then_inc(sig("oh_ready") if (e, b) == (1, 1) else sig("oh_part"), 1)

            def gathered(n, q):
                dve.wait_ge(sig("g_done"), n + 3)
                for h in range(2):
                    ins = dve.tensor_tensor(xg[q][:, 4 * h:4 * h + 4, :], v3(ps[:, h, :], 4),
                                            par_c("norm_ffn_g_2", 4 * h, 4).unsqueeze(2).broadcast_to([P, 4, P]), ALU.mult)
                    ins.then_inc(sig("xg_ready") if h else sig("xg_half"), 1)

            def gate_up(n, q):
                dve.wait_ge(sig("sg_ready"), n + 3)
                dve.tensor_tensor(atok[q], sg[q], ps[:, 2, F_EXP:2 * F_EXP], ALU.mult).then_inc(sig("a_ready"), 1)

            def rows_out(n, q):
                dve.wait_ge(sig("d_done"), n + 3)
                dve.tensor_copy(Yp[q][:, 1, :], ps[:, 2, :]).then_inc(sig("ypb_ready"), 1)

            def dve_step(n, t, q, more=True):
                if more:
                    one_hot(n + 1, t + 1, 1 - q)
                gate_up(n, q)
                if more:
                    gathered(n + 1, 1 - q)
                rows_out(n, q)

            with dve.Fori(0, rounds) as r:
                one_hot(r * NEP, 0, 0)
                gathered(r * NEP, 0)
                dve_step(r * NEP, 0, 0)
                with dve.Fori(0, NEP // 2 - 1) as i:
                    dve_step(r * NEP + i * 2 + 1, i * 2 + 1, 1)
                    dve_step(r * NEP + i * 2 + 2, i * 2 + 2, 0)
                dve_step(r * NEP + NEP - 1, NEP - 1, 1, more=False)
                dve.tensor_scalar(RK, RK, -float(CAP), None, ALU.add).then_inc(sig("rk_down"), 1)
                dve.wait_ge(sig("rk_down"), r + 1)
            dve.wait_ge(sig("moe_done"), 1)
            for b in range(TB):
                dve.tensor_tensor(x_tok[:, b, :], x_tok[:, b, :],
                                  ps[:, 4 + 2 * b:6 + 2 * b, :].rearrange("p a b -> p (a b)"), ALU.add).then_inc(sig("x_ready"), 1)

            norm(4, "norm_ple_g_2")
            for b in range(TB):
                dve.wait_ge(sig("pw_done"), b + 1)
                for half in range(2):
                    dve.wait_ge(sig("sgate_ready"), 2 * b + half + 1)
                    o = (slice(None), b, slice(512 * half, 512 * half + 512))
                    link(dve.tensor_tensor(sgate[o], sgate[o], ps[:, 2 * b + half, :], ALU.mult))
                    last = dve.tensor_tensor(x_tok[o], x_tok[o], sgate[o], ALU.add)
                last.then_inc(sig("x_ready"), 1)
                dve.wait_ge(sig("gbc_landed"), 48)
                dve.wait_ge(sig("std_ready"), 11 + b)
                link(dve.reciprocal(stat[:, 22 + b:23 + b], stat[:, 22 + b:23 + b]))
                dve.scalar_tensor_tensor(hn[:, b, :], x_tok[:, b, :], stat[:, 22 + b:23 + b], gbc[:],
                                         ALU.mult, ALU.mult).then_inc(sig("out_ready"), 1)

        @block.tensor
        def _(pe):
            pe.wait_ge(sig("ident_ready"), 1)
            pe.wait_ge(sig("rows_landed"), 16)
            pe.transpose(ps[:, 7, 0:NROW], prow[0:NROW, :], ident[0:NROW, 0:NROW])
            pe.wait_ge(sig("frow_landed"), 16)
            for t in range(3):
                last = pe.transpose(ps[:, 7, 128 + 44 * t:172 + 44 * t], frow3[:, t, :], ident[0:44, 0:44])
            last.then_inc(sig("par_done"), 1)

            def norm(r):
                for j in range(4):
                    b, h = divmod(j, 2)
                    pe.wait_ge(sig("hn_ready"), 2 * r + b + 1)
                    if j >= 2:
                        pe.wait_ge(sig("hT_ready"), 4 * r + j - 1)
                    for k in range(4):
                        last = pe.transpose(ps[:, h, k * P:(k + 1) * P], hn[:, b, (4 * h + k) * P:(4 * h + k + 1) * P], ident[:])
                    last.then_inc(sig("hT_done"), 1)
                pe.wait_ge(sig("hT_ready"), 4 * r + 4)

            def landed(n):
                pe.wait_ge(sig(f"landed{n % SLOTS}"), 16 * (n // SLOTS + 1))

            def project_T(n, tile, bank, signal, used=False):
                for i in range(2):
                    for k in range(KD):
                        last = pe.matmul(ps[:, bank, 256 * i:256 * i + 256], panel(n)[:, k, (tile + i) * P:(tile + i + 1) * P],
                                         hT[:, k, :], start=(k == 0), stop=(k == KD - 1))
                last.then_inc(sig(signal), 1)

            norm(0)
            pe.wait_ge(sig("params_out"), 3)
            pe.wait_ge(sig("wlr_landed"), 16)
            for d in range(2):
                for k in range(KD):
                    last = pe.matmul(ps[0:RANK, 2, 256 * d:256 * d + 256], wlr[:, k, RANK * d:RANK * (d + 1)], hT[:, k, :],
                                     start=(k == 0), stop=(k == KD - 1))
            last.then_inc(sig("lr_done"), 1)
            landed(0)
            project_T(0, 0, 3, "q_done")
            pe.wait_ge(sig("gup_landed"), 32)
            pe.wait_ge(sig("lr_ready"), at("lr_ready", 1))
            for d in range(2):
                for j in range(2):
                    last = pe.matmul(ps[:, 4 + d, 256 * j:256 * j + 256], gup[0:RANK, d, j * P:(j + 1) * P], lr[0:RANK, d, :],
                                     start=True, stop=True)
                last.then_inc(sig("pre_done"), 1)
            project_T(0, 2, 6, "k_done")
            pe.wait_ge(sig("k_done"), at("k_done", 1))
            pe.sem_inc(sig("panel_used"), 1)
            landed(1)
            for b in range(TB):
                for k in range(KD):
                    last = pe.matmul(ps[:, (7, 2)[b], :], hT[:, k, b * P:(b + 1) * P], panel(1)[:, k, :],
                                     start=(k == 0), stop=(k == KD - 1))
                last.then_inc(sig("v_done"), 1)
            pe.wait_ge(sig("v_done"), at("v_done", 2))
            pe.sem_inc(sig("panel_used"), 1)
            for n, banks, name, free in ((2, (3, 4), "gc", (("q_ready", 1), ("z_ready", 1))),
                                         (3, (5, 6), "gv", (("z_ready", 2), ("k_ready", 1))),
                                         (4, (7, 2), "gb", (("v_ready", 1), ("v_ready", 2))),
                                         (5, (3, 4), "go", (("gc_ready", 1), ("gc_ready", 2)))):
                landed(n)
                for h in range(2):
                    pe.wait_ge(sig(free[h][0]), at(*free[h]))
                    project_T(n, 2 * h, banks[h], name + "_done")
                pe.wait_ge(sig(name + "_done"), at(name + "_done", 2))
                pe.sem_inc(sig("panel_used"), 1)

            for g in range(4):
                b, hh = divmod(g, 2)
                r = 64 * hh
                pe.wait_ge(sig("qk_ready"), at("qk_ready", 4))
                free = (("m_ready", 1), ("m_ready", 2), ("gb_ready", 1), ("gb_ready", 2))[g]
                pe.wait_ge(sig(free[0]), at(*free))
                for j in range(2):
                    for d in range(2):
                        c = 256 * j + b * P
                        last = pe.matmul(ps[:, (5, 6, 7, 2)[g], 256 * j + P * d:256 * j + P * d + P],
                                         k_in[r:r + 64, d, c:c + P], q_in[r:r + 64, d, c:c + P], start=True, stop=True)
                last.then_inc(sig("scores_done"), 1)
            pe.wait_ge(sig("qk_ready"), at("qk_ready", 6))
            for b in range(TB):
                for d in range(2):
                    for j in range(2):
                        o = (2 * d + j) * P
                        last = pe.transpose(ps[:, b, o:o + P], k_out[:, d, 256 * j + b * P:256 * j + b * P + P], ident[:])
                last.then_inc(sig("kot_done"), 1)
            pe.wait_ge(sig("sgo_ready"), at("sgo_ready", 2))
            pe.wait_ge(sig("kot_ready"), at("kot_ready", 2))
            for k in range(3):
                for d in range(2):
                    c = (k, 3 - k)[d]
                    b, r = c // 2, 64 * (c % 2)
                    bank, o = KV_AT[d][k]
                    for j in range(2):
                        for hh in range(2):
                            last = pe.matmul(ps[64 * hh:64 * hh + 64, bank, o + P * j:o + P * j + P],
                                             kot[r:r + 64, b, d, j, 64 * hh:64 * hh + 64],
                                             v_tok[r:r + 64, b, (2 * j + hh) * P:(2 * j + hh + 1) * P], start=True, stop=True)
                last.then_inc(sig("kv_done"), 1)
            pe.wait_ge(sig("PT_ready"), at("PT_ready", 4))
            for b in range(TB):
                for h in range(HEADS):
                    j, hh = divmod(h, 2)
                    o = 256 * b + P * j
                    pe.matmul(ps[:, 6 + hh, o:o + P], PT[:, b, h, :], v_tok[:, b, h * P:(h + 1) * P],
                              start=(j == 0), stop=False, skip_group_check=True)
                if b == 0:
                    pe.wait_ge(sig("S_ready"), 3)
                for c in (2 * b, 2 * b + 1):
                    r = 64 * (c % 2)
                    for d in range(2):
                        k = (c - 1, 2 - c)[d]
                        if k < 0:
                            continue
                        for h in range(HEADS):
                            j, hh = divmod(h, 2)
                            o = 256 * b + P * j
                            last = pe.matmul(ps[r:r + 64, 6 + hh, o:o + P],
                                             q_in[64 * hh:64 * hh + 64, d, 256 * j + c * CH:256 * j + (c + 1) * CH],
                                             S_st[64 * hh:64 * hh + 64, 3 * d + k, j, :],
                                             start=False, stop=True, skip_group_check=True)
                last.then_inc(sig("o_done"), 1)
            for b in range(TB):
                pe.wait_ge(sig("kot_ready"), at("kot_ready", b + 1))
                pe.wait_ge(sig("on_ready"), at("on_ready", b + 1))
                for h in range(HEADS):
                    last = pe.transpose(ps[:, b, h * P:(h + 1) * P], on[:, b, h * P:(h + 1) * P], ident[:])
                last.then_inc(sig("onT_done"), 1)

            def project_tok(n0, signal):
                for b in range(TB):
                    for h in range(2):
                        landed(n0 + h)
                        for k in range(KD):
                            last = pe.matmul(ps[:, 4 + 2 * b + h, :], yT[:, k, b * P:(b + 1) * P], panel(n0 + h)[:, k, :],
                                             start=(k == 0), stop=(k == KD - 1))
                    last.then_inc(sig(signal), 1)

            pe.wait_ge(sig("ya_ready"), at("ya_ready", 1))
            pe.wait_ge(sig("yb_ready"), at("yb_ready", 2))
            project_tok(6, "y_done")
            pe.wait_ge(sig("y_done"), 2)
            pe.sem_inc(sig("panel_used"), 2)
            norm(1)

            pe.wait_ge(sig("x_ready"), 2)
            for n in range(4):
                pe.matmul(ps[:, 4 + n, :], zb[:, 0:P], zb[:], start=True, stop=False, skip_group_check=True)

            def product(o, lhs, rhs, first, last_k):
                pe.matmul(o, lhs[0], rhs[0], start=first, stop=False, skip_group_check=True)
                pe.matmul(o, lhs[0], rhs[1], start=False, stop=False, skip_group_check=True)
                return pe.matmul(o, lhs[1], rhs[0], start=False, stop=last_k, skip_group_check=True)

            def up(p, q):
                if not (isinstance(p, int) and p == 0):
                    pe.wait_ge(sig("tap_done"), p * 8 - 7)
                for c in range(4):
                    pe.wait_ge(sig("up_low"), p * 4 + c + 1)
                    o = ps[:, 2 * q + c // 2, 256 * (c % 2):256 * (c % 2) + 256]
                    for k in range(KD):
                        last = product(o, [t[:, c, k, :] for t in w_up_hl], [t[:, k, :] for t in hT_hl], k == 0, k == KD - 1)
                    last.then_inc(sig("up_used"), 1)

            def down(p, q):
                pe.wait_ge(sig("uact_low"), p + 1)
                for i in range(2):
                    pe.wait_ge(sig("down_low"), p * 2 + i + 1)
                    for b in range(TB):
                        for half in range(2):
                            last = product(ps[:, 4 + 2 * b + half, :], [t[:, q, i, b * P:(b + 1) * P] for t in uact_hl],
                                           [t[:, i, 512 * half:512 * half + 512] for t in w_dn_hl], False, True)
                    last.then_inc(sig("down_used"), 1)

            pe.sem_inc(sig("down_used"), 1)
            pe.wait_ge(sig("hT_low"), 4)
            up(0, 0)
            with pe.Fori(0, NPAIR // 2) as i:
                up(i * 2 + 1, 1)
                down(i * 2, 0)
                up(i * 2 + 2, 0)
                down(i * 2 + 1, 1)
            pe.wait_ge(sig("uact_low"), NPAIR)
            pe.wait_ge(sig("down_low"), 2 * NPAIR)
            for b in range(TB):
                for i in range(2):
                    for half in range(2):
                        last = product(ps[:, 4 + 2 * b + half, :], [t[:, 0, i, b * P:(b + 1) * P] for t in uact_hl],
                                       [t[:, i, 512 * half:512 * half + 512] for t in w_dn_hl], False, True)
                last.then_inc(sig("y_done"), 1)
            pe.wait_ge(sig("y_done"), 4)
            pe.sem_inc(sig("mlp_done"), 2)

            norm(2)
            pe.wait_ge(sig("small_landed"), 16 * 9)
            pe.wait_ge(sig("const2"), 5)
            pe.matmul(ps[64:96, 7, 0:1], invrow[0:1, :], ones[0:1, 0:1], start=True, stop=True).then_inc(sig("icol_done"), 1)
            pe.wait_ge(sig("a2_landed"), 16)
            for b in range(TB):
                for k in range(KD):
                    last = pe.matmul(ps[:, 2 + b, 0:QL + KVL], hT[:, k, b * P:(b + 1) * P], wA[:, k, 0:QL + KVL],
                                     start=(k == 0), stop=(k == KD - 1))
                last.then_inc(sig("c_done"), 1)
            for n in range(2):
                for k in range(KD):
                    last = pe.matmul(ps[0:4, 5, 256 * n:256 * n + 256], wif[:, k, 4 * n:4 * n + 4], hT[:, k, :],
                                     start=(k == 0), stop=(k == KD - 1))
            last.then_inc(sig("if_done"), 1)
            pe.wait_ge(sig("krw_ready"), 2)
            for n in range(2):
                for k in range(KD):
                    w = wA[:, k, C2_KR:C2_KR + ROPE] if n == 0 else krw[:, k, :]
                    last = pe.matmul(ps[64:96, 4, 256 * n:256 * n + 256], w, hT[:, k, :], start=(k == 0), stop=(k == KD - 1))
            last.then_inc(sig("kr_done"), 1)
            pe.wait_ge(sig("kr_done"), at("kr_done", 1))
            pe.sem_inc(sig("a2_used"), 1)

            def tiles(pan, banks, rhs, signal):
                for h in range(2):
                    for i in range(2):
                        for k in range(KD):
                            last = pe.matmul(ps[:, banks[h], 256 * i:256 * i + 256], pan[:, k, (2 * h + i) * P:(2 * h + i + 1) * P],
                                             rhs[:, k, :], start=(k == 0), stop=(k == KD - 1))
                    last.then_inc(sig(signal), 1)

            pe.wait_ge(sig("xm_landed"), 16)
            pe.wait_ge(sig("icol_ready"), at("icol_ready", 1))
            tiles(PAN[0], (6, 7), hT, "xm_done")
            pe.wait_ge(sig("xm_done"), at("xm_done", 2))
            pe.sem_inc(sig("xm_used"), 1)
            pe.wait_ge(sig("cn_ready"), at("cn_ready", 4))
            for b in range(TB):
                for k in range(3):
                    last = pe.transpose(ps[:, b, k * P:(k + 1) * P], cn[:, b, k * P:(k + 1) * P], ident[:])
                last.then_inc(sig("cT_done"), 1)
            pe.wait_ge(sig("zw_landed"), 16)
            tiles(PAN[1], (2, 3), hT, "z2_done")
            pe.wait_ge(sig("z2_done"), at("z2_done", 2))
            pe.sem_inc(sig("zw_used"), 1)
            pe.wait_ge(sig("cT_ready"), at("cT_ready", 2))
            pe.wait_ge(sig("uq_landed"), 32)
            pe.wait_ge(sig("uqw_ready"), 4)
            for hp in range(4):
                bank = 2 * (hp % 2)
                if hp >= 2:
                    pe.wait_ge(sig("qn_ready"), at("qn_ready", hp - 1))
                    pe.wait_ge(sig("qr_ready"), at("qr_ready", hp - 1))
                elif hp == 1:
                    pe.wait_ge(sig("sz_ready"), at("sz_ready", 2))
                for hh in range(2):
                    h = 2 * hp + hh
                    for k in range(2):
                        pe.matmul(ps[0:HQ, bank, 256 * hh:256 * hh + 256], uq[:, k, h * HQ:(h + 1) * HQ], cT[:, k, :],
                                  start=(k == 0), stop=(k == 1))
                    for k in range(2):
                        last = pe.matmul(ps[64:96, bank + 1, 256 * hh:256 * hh + 256], uqw[:, k, h, :], cT[:, k, :],
                                         start=(k == 0), stop=(k == 1))
                last.then_inc(sig("qa_done"), 1)
            for hp in range(4):
                free = (("kr_ready", 1), ("gz_ready", 2), ("xm_ready", 1), ("xm_ready", 2))[hp]
                pe.wait_ge(sig(free[0]), at(*free))
                for hh in range(2):
                    h = 2 * hp + hh
                    last = pe.matmul(ps[0:NOPE, 4 + hp, 256 * hh:256 * hh + 256], ukv[:, h * P:h * P + NOPE], cT[:, 2, :],
                                     start=True, stop=True)
                last.then_inc(sig("ka_done"), 1)
            pe.wait_ge(sig("qn_ready"), at("qn_ready", 3))
            pe.wait_ge(sig("qr_ready"), at("qr_ready", 3))
            for b in range(TB):
                pe.matmul(ps[:, b, :], cT[:, 2, b * P:(b + 1) * P], ukv.rearrange("p (h c) -> p h c", h=A_HEADS)[:, :, NOPE:P],
                          start=True, stop=True).then_inc(sig("v2_done"), 1)
            pe.wait_ge(sig("v2_done"), at("v2_done", 2))
            pe.sem_inc(sig("uq_used"), 1)
            pe.wait_ge(sig("gates_ready"), at("gates_ready", 1))
            pe.wait_ge(sig("qn_ready"), at("qn_ready", 4))
            pe.wait_ge(sig("qr_ready"), at("qr_ready", 4))
            for n, row in ((0, 0), (1, 3)):
                for b in range(TB):
                    o = 8 * n + 4 * b
                    last = pe.transpose(ps[:, 2, o:o + 4], gat[0:4, row, b * P:(b + 1) * P], ident[0:4, 0:4])
            last.then_inc(sig("gT_done"), 1)
            for n in range(2):
                pe.wait_ge(sig("kn_ready"), at("kn_ready", n + 1))
                for i in range(2):
                    last = pe.matmul(ps[:, 4 + n, 256 * i:256 * i + 256], sel4[0:4, 2 * n + i, :], gat[0:4, 1, :],
                                     start=True, stop=True)
                last.then_inc(sig("negM_done"), 1)
            pe.wait_ge(sig("wm_landed"), 48)
            for m, banks, name, src, free in ((0, (6, 7), "mq_done", xcT, "kn_ready"), (1, (0, 1), "mk_done", xcT, "v2_ready")):
                for n in range(2):
                    pe.wait_ge(sig(free), at(free, n + 1 + 2 * (m == 0)))
                    pe.wait_ge(sig("xc_ready"), at("xc_ready", 2 * n + 2))
                    for i in range(2):
                        h = 2 * n + i
                        last = pe.matmul(ps[:, banks[n], 256 * i:256 * i + 256], wm[:, m, h, :], src[:, h, :], start=True, stop=True)
                    last.then_inc(sig(name), 1)
            pe.wait_ge(sig("ucol_ready"), at("ucol_ready", 1))
            for b in range(TB):
                for h in range(M_HEADS):
                    last = pe.matmul(ps[:, 3 - b, h * P:(h + 1) * P], xmT[:, h, 3 + b * P:3 + (b + 1) * P], wm[:, 2, h, :],
                                     start=True, stop=True)
                last.then_inc(sig("mv_done"), 1)
            pe.wait_ge(sig("mv_done"), at("mv_done", 2))
            pe.sem_inc(sig("wm_used"), 1)

            pe.wait_ge(sig("krope_spread"), 1)
            for i in range(10):
                if i < 8:
                    hp, b = divmod(i, 2)
                    nk = P * (b + 1)
                    if i >= 2:
                        pe.wait_ge(sig("s_ready"), i - 1)
                    else:
                        pe.wait_ge(sig("mk_ready"), at("mk_ready", i + 1))
                    for hh in range(2):
                        h = 2 * hp + hh
                        last = pe.matmul(ps[:, i % 2, nk * hh:nk * hh + nk], qTa[0:HQ, h, b * P:(b + 1) * P], kTa[0:HQ, h, 0:nk],
                                         start=True, stop=True)
                    last.then_inc(sig("s_done"), 1)
                h = i // 2
                if i < 8 and i % 2 == 0:
                    if h == 0:
                        pe.wait_ge(sig("mq_ready"), at("mq_ready", 2))
                        pe.wait_ge(sig("mk_ready"), at("mk_ready", 2))
                    else:
                        pe.wait_ge(sig("pm_ready"), h)
                    pe.matmul(ps[:, 6, 0:256], mkT[:, h, 0:P], mqT[:, h, :], start=True, stop=True)
                    pe.matmul(ps[:, 6, 256:384], mkT[:, h, P:SEQ], mqT[:, h, P:SEQ], start=True, stop=True).then_inc(sig("qk_done"), 1)
                if 1 <= i <= 8:
                    g = i - 1
                    b = g % 2
                    pe.wait_ge(sig("p_ready"), g + 1)
                    if g >= 2:
                        pe.wait_ge(sig("PTs_ready"), g - 1)
                    else:
                        pe.wait_ge(sig("mv_ready"), at("mv_ready", 2))
                    for hh in range(2):
                        for kb in range(b + 1):
                            o = ((b + 1) * hh + kb) * P
                            last = pe.transpose(ps[:, 2 + g % 2, o:o + P], sP[g % 2][:, hh, kb * P:(kb + 1) * P], ident[:])
                    last.then_inc(sig("pt_done"), 1)
                if i < 8 and i % 2 == 1:
                    pe.wait_ge(sig("pm_ready"), h + 1)
                    if h >= 1:
                        pe.wait_ge(sig("hm_ready"), h)
                    p_ = pm[h % 2]
                    pe.matmul(ps[:, 7, 0:129], p_[:, 0:P], vext[:, 0, h, :], start=True, stop=True)
                    pe.matmul(ps[:, 7, 129:258], p_[:, P:2 * P], vext[:, 0, h, :], start=True, stop=False)
                    pe.matmul(ps[:, 7, 129:258], p_[:, 2 * P:3 * P], vext[:, 1, h, :], start=False, stop=True).then_inc(sig("num_done"), 1)
                if i >= 2:
                    g = i - 2
                    hp, b = divmod(g, 2)
                    pe.wait_ge(sig("PTs_ready"), g + 1)
                    if g == 0:
                        pe.wait_ge(sig("warg_ready"), 4)
                        pe.wait_ge(sig("warg_all"), 1)
                    if b == 0 and hp >= 2:
                        pe.wait_ge(sig("at_ready"), hp - 1)
                    for hh in range(2):
                        h = 2 * hp + hh
                        for kb in range(b + 1):
                            last = pe.matmul(ps[64 * hh:64 * hh + 64, 4 + hp % 2, b * P:(b + 1) * P],
                                             v2[:, kb, h * VD:(h + 1) * VD], PTs[g % 2][:, (b + 1) * hh + kb, :],
                                             start=(kb == 0), stop=(kb == b), skip_group_check=True)
                    last.then_inc(sig("pv_done"), 1)
            pe.wait_ge(sig("hmn_ready"), at("hmn_ready", 8))
            for b in range(TB):
                for h in range(M_HEADS):
                    last = pe.transpose(ps[:, 6 + b, h * P:(h + 1) * P], hmt[:, b, h * P:(h + 1) * P], ident[:])
                last.then_inc(sig("hmT_done"), 1)
            pe.wait_ge(sig("at_ready"), 4)
            pe.wait_ge(sig("ym_ready"), at("ym_ready", 2))
            for b in range(TB):
                for half in range(2):
                    pe.wait_ge(sig(f"wo{half}_landed"), 16)
                    for k in range(KD):
                        last = pe.matmul(ps[:, 4 + 2 * b + half, :], hT[:, k, b * P:(b + 1) * P], PAN[4 + half][:, k, :],
                                         start=(k == 0), stop=(k == KD - 1))
                last.then_inc(sig("y2_done"), 1)
            pe.wait_ge(sig("y2_done"), at("y2_done", 2))
            pe.sem_inc(sig("wo_used"), 1)
            norm(3)

            for b in range(TB):
                for k in range(KD):
                    last = pe.matmul(ps[:, 2, 36 * b:36 * b + 36], hT[:, k, b * P:(b + 1) * P], wr[:, k, :],
                                     start=(k == 0), stop=(k == KD - 1))
            last.then_inc(sig("logits_done"), 1)
            for k in range(2):
                for b in range(TB):
                    last = pe.transpose(ps[:, 0, 256 * k + P * b:256 * k + P * b + P], ptok[:, b, k * P:(k + 1) * P], ident[:])
            last.then_inc(sig("pT_done"), 1)
            pe.wait_ge(sig("sel_ready"), at("sel_ready", 1))
            pe.matmul(ps[:, 3, 0:32], ustrict, e32[3][:, 0, :], start=True, stop=True)
            pe.matmul(ps[:, 3, 32:64], ones[:], e32[3][:, 0, :], start=True, stop=False)
            pe.matmul(ps[:, 3, 32:64], ustrict, e32[3][:, 1, :], start=False, stop=True)
            pe.matmul(ps[:, 3, 64:96], ones[:], e32[3][:, 0, :], start=True, stop=False)
            pe.matmul(ps[:, 3, 64:96], ones[:], e32[3][:, 1, :], start=False, stop=True).then_inc(sig("rank_done"), 1)
            pe.wait_ge(sig("x_ready"), 6)
            for n in range(4):
                pe.matmul(ps[:, 4 + n, :], zb[:, 0:P], zb[:], start=True, stop=False, skip_group_check=True)

            pe.wait_ge(sig("rounds_ready"), 1)
            rounds = pe.value_load(nri[0:1, :], min_val=1, max_val=SEQ // CAP)
            for name in ("oht_done", "g_done", "u_done", "at_done", "d_done", "scatter_done"):
                pe.sem_inc(sig(name), 2)

            def turn(n, q):
                pe.wait_ge(sig("oh_ready"), n + 3)
                pe.wait_ge(sig("ypa_ready"), n + 1)
                for b in range(TB):
                    last = pe.transpose(ps[:, 3, b * P:(b + 1) * P], OHW[q][:, b, :], ident[:])
                last.then_inc(sig("oht_done"), 1)

            def turn_act(n, q):
                pe.wait_ge(sig("a_ready"), n + 3)
                for f in range(2):
                    last = pe.transpose(ps[:, 3, 256 + f * P:256 + (f + 1) * P], atok[q][:, f * P:(f + 1) * P], ident[:])
                last.then_inc(sig("at_done"), 1)

            def gather(n, q):
                pe.wait_ge(sig("xg_ready"), n + 2)
                for k in range(KD):
                    for b in range(TB):
                        last = pe.matmul(ps[:, k // 4, (k % 4) * P:(k % 4 + 1) * P], hn[:, b, k * P:(k + 1) * P], OH[q][:, b, :],
                                         start=(b == 0), stop=(b == 1))
                last.then_inc(sig("g_done"), 1)

            def expert_up(n, h, q):
                pe.wait_ge(sig("xg_ready"), n + 3)
                pe.wait_ge(sig("ypb_ready"), n + 2)
                for e in range(2):
                    pe.wait_ge(sig(f"gu{e}_landed{q}"), h * 32 + 32)
                for k in range(KD):
                    for e in range(2):
                        last = pe.matmul(ps[CAP * e:CAP * e + CAP, 2, :], xg[q][:, k, CAP * e:CAP * e + CAP],
                                         GU[q][e][:, k, :, :], start=(k == 0), stop=(k == KD - 1))
                last.then_inc(sig("u_done"), 1)
                pe.wait_ge(sig("u_done"), n + 3)
                pe.sem_inc(sig(f"gu0_used{q}"), 1)
                pe.sem_inc(sig(f"gu1_used{q}"), 1)

            def scatter(n, q):
                pe.wait_ge(sig("ypa_ready"), n + 3)
                pe.wait_ge(sig("ypb_ready"), n + 3)
                for b in range(TB):
                    for half in range(2):
                        last = pe.matmul(ps[:, 4 + 2 * b + half, :], SC[q][:, b * P:(b + 1) * P], Yp[q][:, half, :],
                                         start=False, stop=True, skip_group_check=True)
                last.then_inc(sig("scatter_done"), 1)

            def expert_down(n, h, q):
                pe.wait_ge(sig("aT_ready"), n + 3)
                pe.wait_ge(sig(f"de_landed{q}"), h * 16 + 16)
                for half, bank in ((0, 3), (1, 2)):
                    for f in range(2):
                        for e in range(2):
                            last = pe.matmul(ps[CAP * e:CAP * e + CAP, bank, :], aT[q][:, f, CAP * e:CAP * e + CAP],
                                             DE[q][:, e, f, 512 * half:512 * half + 512], start=(f == 0), stop=(f == 1))
                last.then_inc(sig("d_done"), 1)
                pe.wait_ge(sig("d_done"), n + 3)
                pe.sem_inc(sig(f"de_used{q}"), 1)

            def pe_step(n, h, q):
                expert_up(n, h, q)
                scatter(n - 1, 1 - q)
                turn(n + 1, 1 - q)
                turn_act(n, q)
                gather(n + 1, 1 - q)
                expert_down(n, h, q)

            with pe.Fori(0, rounds) as r:
                n0, h0 = r * NEP, r * (NEP // 2)
                turn(n0, 0)
                gather(n0, 0)
                expert_up(n0, h0, 0)
                pe.wait_ge(sig("sc_ready"), n0 + 3)
                turn(n0 + 1, 1)
                turn_act(n0, 0)
                gather(n0 + 1, 1)
                expert_down(n0, h0, 0)
                with pe.Fori(0, NEP // 2 - 1) as i:
                    pe_step(n0 + i * 2 + 1, h0 + i, 1)
                    pe_step(n0 + i * 2 + 2, h0 + i + 1, 0)
                expert_up(n0 + NEP - 1, h0 + NEP // 2 - 1, 1)
                scatter(n0 + NEP - 2, 0)
                turn_act(n0 + NEP - 1, 1)
                expert_down(n0 + NEP - 1, h0 + NEP // 2 - 1, 1)
                scatter(n0 + NEP - 1, 1)
            pe.wait_ge(sig("scatter_done"), rounds * NEP + 2)
            pe.sem_inc(sig("moe_done"), 1)
            for q in range(2):
                for e in range(2):
                    pe.wait_ge(sig(f"gu{e}_landed{q}"), rounds * (NEP * 16) + 32)
                pe.wait_ge(sig(f"de_landed{q}"), rounds * (NEP * 8) + 16)
            pe.sem_inc(sig("slots_free"), 1)

            norm(4)
            pe.wait_ge(sig("pT_ready"), at("pT_ready", 1))
            pe.wait_ge(sig("wple_landed"), 16)
            for b in range(TB):
                for half in range(2):
                    for k in range(2):
                        last = pe.matmul(ps[:, 2 * b + half, :], pT[:, k, b * P:(b + 1) * P], wple[:, k, 512 * half:512 * half + 512],
                                         start=(k == 0), stop=(k == 1))
                last.then_inc(sig("pw_done"), 1)
            for b in range(TB):
                for half in range(2):
                    pe.wait_ge(sig(f"pg{half}_landed"), 16)
                    for k in range(KD):
                        last = pe.matmul(ps[:, 4 + 2 * b + half, :], hT[:, k, b * P:(b + 1) * P], PAN[3 + half][:, k, :],
                                         start=(k == 0), stop=(k == KD - 1))
                    last.then_inc(sig("pg_done"), 1)


_INS = ["x", "norm_mix_post", "norm_ffn_post", "w_in", "gate_up_fwd", "gate_up_bwd", "w_out", "w_up",
        "conv_ffn", "w_down", "p_2", "positions_2", "w_in_2", "w_uq_2", "w_ukv_2", "w_mq_2", "w_mk_2", "w_mv_2",
        "b_igate_2", "b_fgate_2", "w_o_2", "w_router_group_2", "b_router_group_2", "w_router_expert_2",
        "b_router_expert_2", "w_gate_e_2", "w_up_e_2", "w_down_e_2", "w_ple_2", "w_ple_gate_2",
        "final_norm_g_2"]


def kernel(**inputs):
    import numpy as _np
    import concourse.bacc as _bacc
    from concourse import mybir as _mybir
    from concourse.bass_utils import run_bass_kernel_spmd as _run

    nc = _bacc.Bacc("TRN2", target_bir_lowering=False, num_devices=1)
    arrays, args = {}, {}
    laid_out = {name: inputs[name] for name in _INS}
    laid_out["rows"] = _np.concatenate([_np.asarray(inputs[name]).reshape(-1, P) for name, _ in ROWS])
    for name, value in laid_out.items():
        a = _np.ascontiguousarray(value)
        arrays[f"in_{name}_dram"] = a
        args[name] = nc.dram_tensor(f"in_{name}_dram", a.shape, _mybir.dt.from_np(a.dtype), kind="ExternalInput").ap()
    out = nc.dram_tensor("out_0_dram", (1, SEQ, D), F32, kind="ExternalOutput").ap()
    build(nc, args, out)
    r = _run(nc, [arrays], core_ids=[0])
    return r.results[0]["out_0_dram"]
```
